# Optimizing a Trainium2 kernel written in Bass

```python
import math
import jax, jax.numpy as jnp
from jax import lax
import numpy as np

D_MODEL = 1024
BATCH = 1
SEQ = 256
DEPTH = 1
DEC_BATCH = 8
DEC_SEQ = 1
PAST_LEN = 2048
PAGE_SIZE = 128

GDN_HEADS = 8
GDN_DK = 128
GDN_DV = 128
QK_DIM = GDN_HEADS * GDN_DK
V_DIM = GDN_HEADS * GDN_DV
QKV_CH = 2 * QK_DIM + V_DIM
SHORT_CONV = 4
CHUNK = 64
CONF_CH = D_MODEL // 2
CONF_K = 31
N_EXPERTS = 32
TOP_K = 4
D_FF = D_MODEL
SWIGLU_LIMIT = 7.0
SWIGLU_ALPHA = 1.702
PLE_DIM = 256
NORM_EPS = 1e-6
LN_EPS = 1e-5

OFF_Q = 0
OFF_K = OFF_Q + QK_DIM
OFF_V = OFF_K + QK_DIM
OFF_Z = OFF_V + V_DIM
OFF_BETA = OFF_Z + V_DIM
OFF_A = OFF_BETA + GDN_HEADS
OFF_GLU = OFF_A + GDN_HEADS
OFF_GATE = OFF_GLU + 2 * CONF_CH
IN_COLS = OFF_GATE + 2 * D_MODEL

kernel_name = "hybrid_gdn_conformer_moe_step"

def _rmsnorm(x, g):
    xf = x.astype(jnp.float32)
    y = xf * lax.rsqrt(jnp.mean(xf * xf, axis=-1, keepdims=True) + NORM_EPS)
    return (y * g.astype(jnp.float32)).astype(x.dtype)

def _layernorm(x, g, b):
    xf = x.astype(jnp.float32)
    mu = jnp.mean(xf, axis=-1, keepdims=True)
    var = jnp.mean(jnp.square(xf - mu), axis=-1, keepdims=True)
    y = (xf - mu) * lax.rsqrt(var + LN_EPS)
    return (y * g.astype(jnp.float32) + b.astype(jnp.float32)).astype(x.dtype)

def _l2norm(x):
    return x * lax.rsqrt(jnp.sum(x * x, axis=-1, keepdims=True) + NORM_EPS)

def _causal_dwconv(xpad, w):
    c = xpad.shape[-1]
    return lax.conv_general_dilated(xpad, w[:, None, :].astype(xpad.dtype), window_strides=(1,), padding="VALID",
                                    dimension_numbers=("NWC", "WIO", "NWC"), feature_group_count=c)

def _gated_delta_chunked(q, k, v, beta, g, s0):
    b, l, h, _ = q.shape
    c = min(CHUNK, l)
    nc = -(-l // c)
    pad = nc * c - l
    def prep(t):
        t = jnp.pad(t, ((0, 0), (0, pad)) + ((0, 0),) * (t.ndim - 2))
        t = jnp.moveaxis(t, 2, 1)
        return t.reshape((b, h, nc, c) + t.shape[3:])
    qc, kc, vc, bc, gcn = prep(q), prep(k), prep(v), prep(beta), prep(g)
    gc = jnp.cumsum(gcn, axis=-1)
    idx = jnp.arange(c)
    tril = idx[:, None] >= idx[None, :]
    strict = idx[:, None] > idx[None, :]
    decay = jnp.exp(jnp.where(tril, gc[..., :, None] - gc[..., None, :], -jnp.inf))
    kb = kc * bc[..., None]
    a_mat = jnp.where(strict, jnp.einsum("bhncd,bhnsd->bhncs", kb, kc) * decay, 0.0)
    eye = jnp.eye(c, dtype=jnp.float32)
    t_inv = lax.linalg.triangular_solve(eye + a_mat, jnp.broadcast_to(eye, a_mat.shape), left_side=True, lower=True)
    u = jnp.einsum("bhncs,bhnse->bhnce", t_inv, vc * bc[..., None])
    w = jnp.einsum("bhncs,bhnsd->bhncd", t_inv, kb * jnp.exp(gc)[..., None])
    qk = jnp.einsum("bhncd,bhnsd->bhncs", qc, kc) * decay
    qg = qc * jnp.exp(gc)[..., None]
    kd = kc * jnp.exp(gc[..., -1:] - gc)[..., None]
    dl = jnp.exp(gc[..., -1])

    def step(s, inp):
        qg_c, kd_c, u_c, w_c, qk_c, dl_c = inp
        v_new = u_c - jnp.einsum("bhcd,bhde->bhce", w_c, s)
        o = jnp.einsum("bhcd,bhde->bhce", qg_c, s) + jnp.einsum("bhcs,bhse->bhce", qk_c, v_new)
        s = s * dl_c[..., None, None] + jnp.einsum("bhcd,bhce->bhde", kd_c, v_new)
        return s, o

    xs = tuple(jnp.moveaxis(t, 2, 0) for t in (qg, kd, u, w, qk, dl))
    s_fin, o = lax.scan(step, s0.astype(jnp.float32), xs)
    o = jnp.moveaxis(o, 0, 2).reshape(b, h, nc * c, GDN_DV)
    o = jnp.moveaxis(o, 1, 2)[:, :l]
    return o, s_fin

def _moe(x2d, w_router, b_router, w_gate_up, b_gate_up, w_down, b_down):
    logits = x2d.astype(jnp.float32) @ w_router.astype(jnp.float32) + b_router.astype(jnp.float32)
    top_v, top_i = lax.top_k(logits, TOP_K)
    top_w = jax.nn.softmax(top_v, axis=-1)
    gates = jnp.sum(jax.nn.one_hot(top_i, N_EXPERTS, dtype=jnp.float32) * top_w[..., None], axis=1)
    out = jnp.zeros(x2d.shape, jnp.float32)
    for e in range(N_EXPERTS):
        gu = x2d @ w_gate_up[e] + b_gate_up[e]
        gate = jnp.minimum(gu[:, :D_FF], SWIGLU_LIMIT)
        up = jnp.clip(gu[:, D_FF:], -SWIGLU_LIMIT, SWIGLU_LIMIT)
        hid = (up + 1.0) * (gate * jax.nn.sigmoid(SWIGLU_ALPHA * gate))
        ye = hid @ w_down[e] + b_down[e]
        out = out + gates[:, e:e + 1] * ye.astype(jnp.float32)
    return out.astype(x2d.dtype)

def _layer(x, p_l, s0, qkv_buf, conf_buf, norm_mix, w_in, conv_qkv_w, a_log, dt_bias, gdn_norm, w_gdn_out,
           conf_dw_w, conf_dw_b, conf_ln_g, conf_ln_b, w_conf_out, w_out, norm_ffn, w_router, b_router,
           w_gate_up, b_gate_up, w_down, b_down, norm_ple, w_ple_gate, w_ple_proj):
    b, l, _ = x.shape
    a = _rmsnorm(x, norm_mix)
    proj = jnp.einsum("bld,dc->blc", a, w_in)
    qkv_raw = proj[..., :OFF_Z]
    z = proj[..., OFF_Z:OFF_BETA]
    beta_raw = proj[..., OFF_BETA:OFF_A]
    a_raw = proj[..., OFF_A:OFF_GLU]
    glu_in = proj[..., OFF_GLU:OFF_GATE]
    gate_logits = proj[..., OFF_GATE:]

    qkv_pad = jnp.concatenate([qkv_buf.astype(x.dtype), qkv_raw], axis=1)
    new_qkv_buf = qkv_pad[:, -(SHORT_CONV - 1):]
    qkv = jax.nn.silu(_causal_dwconv(qkv_pad, conv_qkv_w)).astype(jnp.float32)
    q = _l2norm(qkv[..., OFF_Q:OFF_K].reshape(b, l, GDN_HEADS, GDN_DK)) * (GDN_DK ** -0.5)
    k = _l2norm(qkv[..., OFF_K:OFF_V].reshape(b, l, GDN_HEADS, GDN_DK))
    v = qkv[..., OFF_V:OFF_Z].reshape(b, l, GDN_HEADS, GDN_DV)
    beta = jax.nn.sigmoid(beta_raw.astype(jnp.float32))
    g = -jnp.exp(a_log.astype(jnp.float32)) * jax.nn.softplus(a_raw.astype(jnp.float32) + dt_bias.astype(jnp.float32))
    o, s_new = _gated_delta_chunked(q, k, v, beta, g, s0)
    o = o * lax.rsqrt(jnp.mean(o * o, axis=-1, keepdims=True) + NORM_EPS) * gdn_norm.astype(jnp.float32)
    o = o * jax.nn.silu(z.astype(jnp.float32).reshape(b, l, GDN_HEADS, GDN_DV))
    branch_a = jnp.einsum("blc,cd->bld", o.reshape(b, l, V_DIM).astype(x.dtype), w_gdn_out)

    u = glu_in[..., :CONF_CH] * jax.nn.sigmoid(glu_in[..., CONF_CH:])
    u_pad = jnp.concatenate([conf_buf.astype(x.dtype), u], axis=1)
    new_conf_buf = u_pad[:, -(CONF_K - 1):]
    cv = _causal_dwconv(u_pad, conf_dw_w) + conf_dw_b
    cv = jax.nn.silu(_layernorm(cv, conf_ln_g, conf_ln_b))
    branch_b = jnp.einsum("blc,cd->bld", cv, w_conf_out)

    g_a = jax.nn.sigmoid(gate_logits[..., :D_MODEL])
    g_b = jax.nn.sigmoid(gate_logits[..., D_MODEL:])
    x = x + jnp.einsum("bld,de->ble", g_a * branch_a + g_b * branch_b, w_out)

    hm = _rmsnorm(x, norm_ffn).reshape(b * l, D_MODEL)
    x = x + _moe(hm, w_router, b_router, w_gate_up, b_gate_up, w_down, b_down).reshape(b, l, D_MODEL)

    gate = jax.nn.sigmoid(jnp.einsum("bld,de->ble", _rmsnorm(x, norm_ple), w_ple_gate))
    x = x + jnp.einsum("blp,pd->bld", p_l, w_ple_proj) * gate
    return x, s_new, new_qkv_buf, new_conf_buf

def setup_inputs(seed: int = 0) -> dict:
    key = jax.random.key(seed)
    ks = jax.random.split(key, 40)
    f32 = jnp.float32
    def nrm(i, shape, scale):
        return jax.random.normal(ks[i], shape, f32) * scale
    def gain(i, shape):
        return 1.0 + 0.02 * jax.random.normal(ks[i], shape, f32)
    return {
        "x_prompt": nrm(0, (BATCH, SEQ, D_MODEL), 1.0),
        "x_sample": nrm(1, (DEC_BATCH, DEC_SEQ, D_MODEL), 1.0),
        "p_prompt": nrm(2, (DEPTH, BATCH, SEQ, PLE_DIM), 1.0),
        "p_sample": nrm(3, (DEPTH, DEC_BATCH, DEC_SEQ, PLE_DIM), 1.0),
        "state_gdn": nrm(4, (DEPTH, DEC_BATCH, GDN_HEADS, GDN_DK, GDN_DV), GDN_DK ** -0.5),
        "state_qkv_conv": nrm(5, (DEPTH, DEC_BATCH, SHORT_CONV - 1, QKV_CH), 1.0),
        "state_conf_conv": nrm(6, (DEPTH, DEC_BATCH, CONF_K - 1, CONF_CH), 0.5),
        "norm_mix": gain(7, (DEPTH, D_MODEL)),
        "w_in": nrm(8, (DEPTH, D_MODEL, IN_COLS), D_MODEL ** -0.5),
        "conv_qkv_w": nrm(9, (DEPTH, SHORT_CONV, QKV_CH), SHORT_CONV ** -0.5),
        "a_log": jnp.log(jax.random.uniform(ks[10], (DEPTH, GDN_HEADS), f32, 1.0, 16.0)),
        "dt_bias": nrm(11, (DEPTH, GDN_HEADS), 0.1) - 2.0,
        "gdn_norm": gain(12, (DEPTH, GDN_DV)),
        "w_gdn_out": nrm(13, (DEPTH, V_DIM, D_MODEL), V_DIM ** -0.5),
        "conf_dw_w": nrm(14, (DEPTH, CONF_K, CONF_CH), CONF_K ** -0.5),
        "conf_dw_b": nrm(15, (DEPTH, CONF_CH), 0.02),
        "conf_ln_g": gain(16, (DEPTH, CONF_CH)),
        "conf_ln_b": nrm(17, (DEPTH, CONF_CH), 0.02),
        "w_conf_out": nrm(18, (DEPTH, CONF_CH, D_MODEL), CONF_CH ** -0.5),
        "w_out": nrm(19, (DEPTH, D_MODEL, D_MODEL), D_MODEL ** -0.5),
        "norm_ffn": gain(20, (DEPTH, D_MODEL)),
        "w_router": nrm(21, (DEPTH, D_MODEL, N_EXPERTS), D_MODEL ** -0.5),
        "b_router": nrm(22, (DEPTH, N_EXPERTS), 0.01),
        "w_gate_up": nrm(23, (DEPTH, N_EXPERTS, D_MODEL, 2 * D_FF), D_MODEL ** -0.5),
        "b_gate_up": nrm(24, (DEPTH, N_EXPERTS, 2 * D_FF), 0.02),
        "w_down": nrm(25, (DEPTH, N_EXPERTS, D_FF, D_MODEL), D_FF ** -0.5),
        "b_down": nrm(26, (DEPTH, N_EXPERTS, D_MODEL), 0.02),
        "norm_ple": gain(27, (DEPTH, D_MODEL)),
        "w_ple_gate": nrm(28, (DEPTH, D_MODEL, D_MODEL), D_MODEL ** -0.5),
        "w_ple_proj": nrm(29, (DEPTH, PLE_DIM, D_MODEL), PLE_DIM ** -0.5),
        "norm_final": gain(30, (D_MODEL,)),
    }

def reference(x_prompt, x_sample, p_prompt, p_sample, state_gdn, state_qkv_conv, state_conf_conv,
              norm_mix, w_in, conv_qkv_w, a_log, dt_bias, gdn_norm, w_gdn_out, conf_dw_w, conf_dw_b,
              conf_ln_g, conf_ln_b, w_conf_out, w_out, norm_ffn, w_router, b_router, w_gate_up, b_gate_up,
              w_down, b_down, norm_ple, w_ple_gate, w_ple_proj, norm_final):
    hp, hs = x_prompt, x_sample
    bp = x_prompt.shape[0]
    sp_l, qp_l, cp_l, ss_l, qs_l, cs_l = [], [], [], [], [], []
    for i in range(DEPTH):
        lp = (norm_mix[i], w_in[i], conv_qkv_w[i], a_log[i], dt_bias[i], gdn_norm[i], w_gdn_out[i],
              conf_dw_w[i], conf_dw_b[i], conf_ln_g[i], conf_ln_b[i], w_conf_out[i], w_out[i], norm_ffn[i],
              w_router[i], b_router[i], w_gate_up[i], b_gate_up[i], w_down[i], b_down[i], norm_ple[i],
              w_ple_gate[i], w_ple_proj[i])
        s0 = jnp.zeros((bp, GDN_HEADS, GDN_DK, GDN_DV), jnp.float32)
        q0 = jnp.zeros((bp, SHORT_CONV - 1, QKV_CH), x_prompt.dtype)
        c0 = jnp.zeros((bp, CONF_K - 1, CONF_CH), x_prompt.dtype)
        hp, sp, qp, cp = _layer(hp, p_prompt[i], s0, q0, c0, *lp)
        hs, ss, qs, cs = _layer(hs, p_sample[i], state_gdn[i], state_qkv_conv[i], state_conf_conv[i], *lp)
        sp_l.append(sp); qp_l.append(qp); cp_l.append(cp)
        ss_l.append(ss); qs_l.append(qs); cs_l.append(cs)
    y_prompt = _rmsnorm(hp, norm_final)
    y_sample = _rmsnorm(hs, norm_final)
    return (y_prompt, y_sample, jnp.stack(sp_l), jnp.stack(qp_l), jnp.stack(cp_l),
            jnp.stack(ss_l), jnp.stack(qs_l), jnp.stack(cs_l))


_drawn_inputs = setup_inputs


def setup_inputs(seed=0):
    import zlib

    import numpy as np

    out = dict(_drawn_inputs(seed))
    spreads = {}
    factors = {'gdn_norm': 7.784,
     'conf_ln_g': 3.058,
     'b_router': 2.765,
     'b_gate_up': 5.896,
     'b_down': 6.777,
     'norm_ple': 64.0,
     'norm_final': 7.564,
     'conf_ln_b': 5.434}
    for name, (base, spread) in spreads.items():
        noise = np.random.default_rng([zlib.crc32(name.encode()), seed]).standard_normal(out[name].shape)
        drawn = base * np.exp(spread * noise) if base else spread * noise
        out[name] = __import__('jax').numpy.asarray(drawn.astype(out[name].dtype))
    for name, factor in factors.items():
        out[name] = (out[name] * factor).astype(out[name].dtype)
    return out
```

```python
import concourse.bass as bass
from concourse import mybir
from contextlib import ExitStack

FP32 = mybir.dt.float32
INT32 = mybir.dt.int32
ALU = mybir.AluOpType
ACT = mybir.ActivationFunctionType
AX = mybir.AxisListType

P = 128
D = 1024
KD = D // P
TP, TS = 256, 8
T = TP + TS
H = 8
HIST = 3
CC = 512
CB = CC // P
CK = 31
QKV = 3 * D
OFF_Z, OFF_BETA, OFF_A, OFF_GLU, OFF_GATE = 3072, 4096, 4104, 4112, 5136
NE, TOPK = 32, 4
PLE = 256
NORM_EPS, LN_EPS = 1e-6, 1e-5
LIMIT, ALPHA = 7.0, 1.702
PARAM_DMAS, ROW_DMAS = 13, 7
CONSTS = 3
CAP = 96
PASSES = -(-T // CAP)
TB = 88
NTB = T // TB
CHUNK = 128
LEVELS = [2, 4, 8, 16, 32]
BIG = 3.0e38

CHUNK_COLS = 2048
RING_A = 6
RING_E = 12

GLU_ORDER = [("val", 0), ("val", 1), ("sig", 0), ("sig", 1), ("val", 2), ("val", 3), ("sig", 2), ("sig", 3)]
QKV_ORDER = [(kind, 2 * g + j) for g in range(4) for kind in range(3) for j in range(2)]


def _column_blocks():
    out = [(k, i, OFF_GLU + (CC if k == "sig" else 0) + P * i) for k, i in GLU_ORDER]
    out += [("qkv", n, kind * D + h * P) for n, (kind, h) in enumerate(QKV_ORDER)]
    out += [("z", h, OFF_Z + P * h) for h in range(H)]
    out += [("ga", i, OFF_GATE + P * i) for i in range(KD)]
    out += [("gb", i, OFF_GATE + D + P * i) for i in range(KD)]
    return out


BLOCKS = _column_blocks()
N_BLOCKS = len(BLOCKS)
FIRST_GDN_BLOCK = 16

GDN_STEPS = ["norm", "bcast", "scores", "tokens"]
for _lv in range(len(LEVELS)):
    GDN_STEPS += [f"ad{_lv}", f"dm{_lv}", f"tr{_lv}"]
GDN_STEPS += ["adl", "lt", "vn0", "s1", "ks", "vn1", "s2", "o", "onorm"]
GDN_JOBS = {"norm": ["n0", "n1", "n2", "n3"], "bcast": ["bcg0", "bcb0", "bcg1", "bcb1"],
            "scores": ["AT", "QK"], "tokens": ["kt", "vt", "T1"], "onorm": ["on0", "on1"]}
SAMPLE_STEPS = {"ad0": ("skq", 0), "ad1": ("srow", 0), "ad2": ("kv", 0),
                "ad3": ("skq", 1), "ad4": ("srow", 1), "adl": ("kv", 1)}


def _timetable():
    out = []
    gdn = [(g, step) for g in range(4) for step in GDN_STEPS]
    for n in range(N_BLOCKS + 1):
        for third in range(3):
            out.append(("block", n, third))
            if n >= FIRST_GDN_BLOCK and gdn:
                out.append(("gdn", *gdn.pop(0)))
            if third == 1:
                if n in (12, 13):
                    out.append(("conf_rows", n - 12, 0))
                if 34 <= n < 40:
                    out.append(("tail", n - 34, 0))
                if n == 50:
                    out.append(("conf_mean", 0, 0))
                if n == 52:
                    out.append(("conf_var", 0, 0))
            if n >= 12:
                out.append(("conf_tap", n, third))
    return out


TIMETABLE = _timetable()
CONF_SLOTS = [(i[1], i[2]) for i in TIMETABLE if i[0] == "conf_tap" and i[1] < 48]
TAPS_A_SLOT = -(-CK * CB // len(CONF_SLOTS))

SEMAPHORES = """consts x_loaded params_loaded ba_loaded late_loaded bd_loaded rows_loaded squares rstd_ready aT_ready
 act_order dve_order pool_order conv_ready silu_sig qkv_ready sample_acc sample_sig u_ready z_sig
 gates_in e1_ready sp_in ln_ready expa gT_ready esc_in esc_ready gcF_ready nsq nrstd nrm dec_diff
 dec_exp kb_ready kbg_ready DT0_ready osq_ready orstd_ready onorm_ready kq_ready sample_ready
 state_loaded0 state_loaded1 svn_ready os_ready sscaled state_stored0 state_stored1 sfin_stored
 masks_ready conf_done csq crstd caff csig cv_ready mix tail_stored nmax wexp gates
 selected rank flag_ready outs x3""".split()

EXPERT_SEMAPHORES = """onehot gated gather_filled xsel gate_in gate_sig hid yT yt_filled ysb
 sc_filled sc_added pt_filled pgT chunk_used dve_e""".split()


class Teller:

    def __init__(self, engine, sems, own):
        self.engine, self.sems, self.own = engine, sems, own
        self.count = {}

    def __call__(self, instruction, name=None):
        name = name or self.own
        self.count[name] = self.count.get(name, 0) + 1
        instruction.then_inc(self.sems[name], 1)
        self.engine.wait_ge(self.sems[name], self.count[name])


def build(nc, a, out):
    with ExitStack() as ctx:
        def sbuf(name, shape, dt=FP32):
            return ctx.enter_context(nc.sbuf_tensor(name, shape, dt))

        s = {n: ctx.enter_context(nc.semaphore(n)) for n in SEMAPHORES}
        first = {n: ctx.enter_context(nc.semaphore("e_" + n)) for n in EXPERT_SEMAPHORES}
        more = {n: ctx.enter_context(nc.semaphore("m_" + n)) for n in EXPERT_SEMAPHORES}
        loaded = [ctx.enter_context(nc.semaphore(f"slot_loaded_{i}")) for i in range(RING_E)]
        more_loaded = [ctx.enter_context(nc.semaphore(f"slot_loaded_more_{i}")) for i in range(RING_E)]
        filled = [ctx.enter_context(nc.semaphore(f"bank_filled_{i}")) for i in range(8)]
        drained = [ctx.enter_context(nc.semaphore(f"bank_drained_{i}")) for i in range(8)]

        ring = sbuf("ring", [P, RING_E, CHUNK_COLS])
        upper = ring[:, RING_A:RING_E, :].rearrange("p s c -> p (s c)")

        def carve(base, start, *shape):
            n = 1
            for x in shape:
                n *= x
            v = base[:, start:start + n]
            if len(shape) == 2:
                v = v.rearrange("p (a b) -> p a b", a=shape[0])
            elif len(shape) == 3:
                v = v.rearrange("p (a b c) -> p a b c", a=shape[0], b=shape[1])
            return v

        qkvT = carve(upper, 0, 24, T)
        at = 24 * T
        AT = carve(upper, at, 4, P)
        Dm = carve(upper, at + 512, 4, P)
        DT = carve(upper, at + 1024, 4, P)
        M = carve(upper, at + 1536, 4, P)
        QKT = carve(upper, at + 2048, 4, P)
        kd = carve(upper, at + 2560, 4, P)
        vb = carve(upper, at + 3072, 4, P)
        dec = carve(upper, at + 3584, 4, P)
        kb = carve(upper, at + 4096, 2, T)
        kbg = carve(upper, at + 4096 + 528, 2, T)
        qg = carve(upper, at + 4096 + 1056, 2, T)
        S1 = carve(upper, at + 4096 + 1584, 2, P)
        osq = kb
        nsq = carve(upper, at + 4096, 4, T)
        nstd = carve(upper, at, 4, T)
        vn = M
        xs = carve(upper, at, 3, D)
        ps_tok = carve(upper, at + 3072, 3, PLE)
        stage = carve(upper, at + 3072 + 768, 3, P)

        big = sbuf("big", [P, 3 * KD * T])
        zT = carve(big, 0, H, T)
        gaT = carve(big, KD * T, KD, T)
        gbT = carve(big, 2 * KD * T, KD, T)
        hist_rows = big[0:TS * HIST, 0:QKV]
        bgu_rows = big[0:NE, QKV:QKV + 2 * D]
        conf_rows = carve(big, QKV + 2 * D, 2, CC)
        hm_tok = carve(big, 0, NTB, D)
        xsel, gbuf, ubuf, sbuf_sig = (carve(big, NTB * D + i * KD * CAP, KD, CAP) for i in range(4))

        xT = sbuf("xT", [P, KD, T])
        aT = sbuf("aT", [P, KD, T])
        oT = sbuf("oT", [P, H, T])
        yT = carve(aT[:].rearrange("p k t -> p (k t)"), 0, KD, CAP)
        cv = sbuf("cv", [P, CB, T])
        conf = sbuf("conf", [P, CB * 286 + CB * 248])
        up = carve(conf, 0, CB, 286)
        us = carve(conf, CB * 286, CB, TS, CK)
        conf_sq = carve(conf, 0, CB, T)
        b_down = carve(conf, 0, D)
        pieces = sbuf("pieces", [P, 5, T])
        raw = pieces[:, 0, :]
        acc = pieces[:, 1, :]
        sig = pieces[:, 2, :]
        vals = [pieces[:, 3, :], pieces[:, 4, :]]
        hist = sbuf("hist", [P, 24, TS * HIST])
        tail = sbuf("tail", [P, 24, 11])
        sacc = sbuf("sacc", [P, 6, TS])
        stmp = sbuf("stmp", [P, 6, TS])
        par = sbuf("par", [P, 45])
        wconv = sbuf("wconv", [P, 4, 24])
        wdw = sbuf("wdw", [P, CK, CB])
        ident = sbuf("ident", [P, P])
        ones = sbuf("ones", [P, P])
        causal = sbuf("causal", [P, P])
        neg_first = sbuf("neg_first", [P, P])
        neg_mask = sbuf("neg_mask", [P, len(LEVELS) + 1, P])
        sel8 = sbuf("sel8", [H, H, P])
        bguT = sbuf("bguT", [P, 16, NE])
        rows8 = sbuf("rows8", [H, 2, T])
        betaT, gcF = rows8[:, 0, :], rows8[:, 1, :]
        gT, tmp8, tmp8b = acc[0:H], vals[0][0:H], vals[1][0:H]
        small8 = sbuf("small8", [H, 4])
        gbt = sbuf("gbt", [P, 4, H])
        gct = sbuf("gct", [P, 4, H])
        esc = sbuf("esc", [P, 4, H])
        eg = sbuf("eg", [P, 2, T])
        beta_s = sbuf("beta_s", [P, 2, TS])
        kq = sbuf("kq", [P, 2, TS, 2])
        qk_s = sbuf("qk_s", [P, 2, TS])
        sv = sbuf("sv", [P, 4, TS])
        rstd = sbuf("rstd", [P, T])
        ostd = sbuf("ostd", [P, 2, T])
        st = sbuf("st", [P, 2, TS, P])
        krow = sbuf("krow", [TS, P])
        vbd = sbuf("vbd", [TS, TS, P])
        sfin = sbuf("sfin", [P, 2, P])
        qrow = sbuf("qrow", [CK - 1, 4 * P])
        pT = sbuf("pT", [P, 2, T])
        wr = sbuf("wr", [P, KD, NE])
        wba = sbuf("wba", [P, KD, 2 * H])
        brt = sbuf("brt", [TB, NE])
        eps = sbuf("eps", [P, 2])
        flag = sbuf("flag", [1, 1], INT32)
        slots = st[:].rearrange("p a b c -> p (a b c)")
        at = [0]

        def small(*shape):
            v = carve(slots, at[0], *shape)
            n = 1
            for x in shape:
                n *= x
            at[0] += n + n % 2
            return v

        lg, rep = small(NTB, NE + TOPK)[0:TB], small(NTB, NE + TOPK)[0:TB]
        m8 = small(NTB, 8)[0:TB]
        nmax, wsum = small(NTB)[0:TB], small(NTB)[0:TB]
        sel, gates = small(NTB, NE)[0:TB], small(NTB, NE)[0:TB]
        rank = small(NTB, PASSES * NE)[0:TB]
        onehot, gated = small(NTB, CAP)[0:TB], small(NTB, CAP)[0:TB]
        iota, iota_int = small(CAP)[0:TB], small(CAP)[0:TB].bitcast(INT32)
        cnt, cmax = small(NE), small(1)
        gatesT = small(T)[0:NE]
        before = small(TB)[0:TB]
        assert at[0] <= 2 * TS * P
        ysb = oT[:].rearrange("p a b -> p (a b)")[0:CAP, 0:D]
        pgT = oT[:].rearrange("p a b -> p (a b)")[0:CAP, D:D + T]
        yrows = big[:, 0:3 * D].rearrange("p (t d) -> p t d", t=3)

        bank = [ctx.enter_context(nc.psum_tensor(f"bank{i}", [P, 512], FP32)) for i in range(8)]

        uses = {}
        count = [0] * 8
        turn = [0]

        def plan(name, b):
            uses[name] = (b, count[b])
            count[b] += 1

        early = ["par0", "par1", "par2"] + [f"x{t}{h}" for t in range(3) for h in range(2)]
        early += ["rms1", "bgu", "hist0", "hist1", "ch0", "ch1", "pT", "pTs", "beta", "a", "gbt", "gct", "gcf"]
        for i, n in enumerate(early):
            plan(n, 2 + i % 6)
        for kind, n, x in TIMETABLE:
            if kind == "block" and x == 0 and n < N_BLOCKS:
                plan(f"proj{n}", n % 2)
            elif kind == "gdn":
                for job in GDN_JOBS.get(x, [x]):
                    plan(f"{job}.{n}", 2 + turn[0] % 4)
                    turn[0] += 1
                if x in SAMPLE_STEPS:
                    step, j = SAMPLE_STEPS[x]
                    if step == "kv":
                        plan(f"kv0.{2 * n + j}", 6)
                        plan(f"kv1.{2 * n + j}", 7)
                    else:
                        plan(f"{step}.{2 * n + j}", 6 if step == "skq" else 7)
            elif kind == "conf_rows":
                plan(f"crow{n}", 6 + n)
            elif kind == "tail":
                plan(f"tail{n}", 6 + n % 2)
            elif kind == "conf_mean":
                plan("cmu", 6)
            elif kind == "conf_var":
                plan("cvar", 7)
        for name in ("bb", "ba", "wo"):
            for i in range(KD):
                plan(f"{name}{i}", i)
        plan("rms2", 0)
        plan("logits", 1)
        for i in range(6):
            plan(f"hm{i}", 2 + i)
        plan("gTr", 0)
        plan("rank", 1)
        for i in range(KD):
            plan(f"bd{i}", i)
        before_experts = list(count)
        plan("rms3", 0)
        for i in range(KD):
            plan(f"pg{i}", 4 * (i % 2) + 1)
            plan(f"pp{i}", 4 * (i % 2) + 2)
        plan("rms4", 0)
        for t in range(3):
            for h in range(2):
                plan(f"y{t}{h}", 2 + 2 * t + h)

        def to_fill(pe, name):
            b, k = uses[name]
            if k:
                pe.wait_ge(drained[b], k)
            return bank[b][:]

        def fill_done(name, instruction):
            instruction.then_inc(filled[uses[name][0]], 1)

        def to_drain(engine, name):
            b, k = uses[name]
            engine.wait_ge(filled[b], k + 1)
            return bank[b][:]

        def drain_sem(name):
            return drained[uses[name][0]]

        def wait_drained(engine, name):
            b, k = uses[name]
            engine.wait_ge(drained[b], k + 1)

        w_in = a["w_in"][0]

        def cols(w, c0, n=256):
            return w[:, c0:c0 + n].rearrange("(k p) c -> p k c", p=P)

        stream = [("in", BLOCKS[2 * i][2]) for i in range(N_BLOCKS // 2)]
        stream += [("conf", i) for i in range(2)] + [("gdn", i) for i in range(4)] + [("out", i) for i in range(4)]
        first_use = {}
        for n, (kind, i) in enumerate(stream):
            first_use[(kind, i)] = n
        slot_fills = [len(range(i, len(stream), RING_A)) for i in range(RING_A)] + [0] * (RING_E - RING_A)

        def chunk_view(kind, slot):
            v = ring[:, slot, :]
            k = {"in": KD, "gdn": KD, "out": KD, "conf": CB, "down": 2}[kind]
            return v.rearrange("p (k c) -> p k c", k=k)

        def take_chunk(pe, kind, i):
            n = first_use[(kind, i)]
            pe.wait_ge(loaded[n % RING_A], 16 * (n // RING_A + 1))
            return chunk_view(kind, n % RING_A)

        def wait_used(engine, n):
            kind, i = stream[n]
            if kind == "in":
                name = f"proj{2 * n + 1}"
            else:
                name = {"conf": f"bb{4 * i + 3}", "gdn": f"ba{2 * i + 1}", "out": f"wo{2 * i + 1}"}[kind]
            to_drain(engine, name)

        block = ctx.enter_context(nc.Block())

        @block.sync
        def _(sp):
            sp.dma_start(wba[:], w_in[:, OFF_BETA:OFF_GLU].rearrange("(k p) c -> p k c", p=P)).then_inc(s["ba_loaded"], 16)
            sp.dma_start(wr[:], a["w_router"][0].rearrange("(k p) c -> p k c", p=P)).then_inc(s["ba_loaded"], 16)
            for n, (kind, i) in enumerate(stream):
                slot = n % RING_A
                if n >= RING_A:
                    wait_used(sp, n - RING_A)
                if kind == "in":
                    src = cols(w_in, i)
                elif kind == "conf":
                    src = cols(a["w_conf_out"][0], 512 * i, 512)
                elif kind == "gdn":
                    src = cols(a["w_gdn_out"][0], 256 * i)
                else:
                    src = cols(a["w_out"][0], 256 * i)
                sp.dma_start(chunk_view(kind, slot), src).then_inc(loaded[slot], 16)

            w_gu, w_dn = a["w_gate_up"][0], a["w_down"][0]

            def load_expert(e, n, sems, sm, skip_wait):
                for c in range(RING_E):
                    if not skip_wait:
                        sp.wait_ge(sm["chunk_used"], n * RING_E + (c + 1 - RING_E))
                    if c < KD:
                        sp.dma_start(ring[:, c, :], w_gu[e, c * P:(c + 1) * P, :]).then_inc(sems[c], 16)
                    else:
                        r = 2 * P * (c - KD)
                        sp.dma_start(chunk_view("down", c),
                                     w_dn[e, r:r + 2 * P, :].rearrange("(k p) d -> p k d", p=P)).then_inc(sems[c], 16)

            for c in range(RING_E):
                if c < RING_A:
                    wait_used(sp, len(stream) - RING_A + (c - len(stream)) % RING_A)
                elif c == RING_A:
                    wait_drained(sp, "o.3")
                    wait_drained(sp, "s2.3")
                    sp.wait_ge(s["os_ready"], H)
                    sp.wait_ge(s["kbg_ready"], H)
                    sp.wait_ge(s["onorm_ready"], 4)
                if c < KD:
                    sp.dma_start(ring[:, c, :], w_gu[0, c * P:(c + 1) * P, :]).then_inc(loaded[c], 16)
                else:
                    r = 2 * P * (c - KD)
                    sp.dma_start(chunk_view("down", c),
                                 w_dn[0, r:r + 2 * P, :].rearrange("(k p) d -> p k d", p=P)).then_inc(loaded[c], 16)
            with sp.Fori(1, NE) as e:
                load_expert(e, e, loaded, first, False)
            sp.wait_ge(s["flag_ready"], 1)
            most = sp.value_load(flag[0:1, 0:1], min_val=0, max_val=T)
            with sp.If(most > CAP):
                sp.wait_ge(first["chunk_used"], NE * RING_E)
                load_expert(0, 0, more_loaded, more, True)
                with sp.Fori(1, NE) as e:
                    load_expert(e, e, more_loaded, more, False)
                with sp.Fori(2, PASSES) as j:
                    with sp.Fori(0, NE) as e:
                        load_expert(e, (j - 1) * NE + e, more_loaded, more, False)
                sp.wait_ge(more["chunk_used"], (PASSES - 1) * NE * RING_E)
            for c in range(5):
                sp.wait_ge(first["chunk_used"], (NE - 1) * RING_E + c + 1)
                if c < 4:
                    sp.dma_start(chunk_view("in", c), cols(a["w_ple_gate"][0], 256 * c)).then_inc(s["late_loaded"], 16)
                else:
                    sp.dma_start(chunk_view("down", c),
                                 a["w_ple_proj"][0].rearrange("(k p) d -> p k d", p=P)).then_inc(s["late_loaded"], 16)

        def q_of(g, j):
            return qkvT[:, 6 * g + j, :]

        def k_of(g, j):
            return qkvT[:, 6 * g + 2 + j, :]

        def v_of(g, j):
            return qkvT[:, 6 * g + 4 + j, :]

        def chunk(v, c):
            return v[:, c * CHUNK:(c + 1) * CHUNK]

        @block.tensor
        def _(pe):
            mm, tr = nc.tensor.matmul, nc.tensor.transpose

            pe.wait_ge(s["consts"], CONSTS)
            pe.wait_ge(s["params_loaded"], 16 * PARAM_DMAS)
            for i, rows in enumerate((45, 96, 124)):
                b = to_fill(pe, f"par{i}")
                fill_done(f"par{i}", tr(b[:, 0:rows], stage[0:rows, i, :], ident[0:rows, 0:rows]))
            pe.wait_ge(s["x_loaded"], 16 * 3)
            for t in range(3):
                w = P if t < 2 else TS
                for h in range(2):
                    b = to_fill(pe, f"x{t}{h}")
                    for i in range(4):
                        k = 4 * h + i
                        last = tr(b[:, i * w:(i + 1) * w], xs[0:w, t, k * P:(k + 1) * P], ident[0:w, 0:w])
                    fill_done(f"x{t}{h}", last)

            def sum_squares(name, n):
                pe.wait_ge(s["squares"], n)
                b = to_fill(pe, name)
                for k in range(KD):
                    last = mm(b[:, 0:T], ones[:], aT[:, k, :], start=k == 0, stop=k == KD - 1)
                fill_done(name, last)

            sum_squares("rms1", 1)
            pe.wait_ge(s["rows_loaded"], 16 * ROW_DMAS)
            b = to_fill(pe, "bgu")
            for k in range(16):
                last = tr(b[:, k * NE:(k + 1) * NE], bgu_rows[:, k * P:(k + 1) * P], ident[0:NE, 0:NE])
            fill_done("bgu", last)
            R = TS * HIST
            for i in range(2):
                b = to_fill(pe, f"hist{i}")
                for m in range(12):
                    kind, h = QKV_ORDER[12 * i + m]
                    c0 = kind * D + h * P
                    last = tr(b[:, m * R:(m + 1) * R], hist_rows[:, c0:c0 + P], ident[0:R, 0:R])
                fill_done(f"hist{i}", last)
            for i in range(2):
                b = to_fill(pe, f"ch{i}")
                for m in range(CB):
                    last = tr(b[:, m * 120:(m + 1) * 120], conf_rows[0:120, i, m * P:(m + 1) * P], ident[0:120, 0:120])
                fill_done(f"ch{i}", last)
            b = to_fill(pe, "pT")
            for t in range(2):
                for k in range(2):
                    last = tr(b[:, k * TP + t * P:k * TP + (t + 1) * P], ps_tok[:, t, k * P:(k + 1) * P], ident[:])
            fill_done("pT", last)
            b = to_fill(pe, "pTs")
            for k in range(2):
                last = tr(b[:, k * TS:(k + 1) * TS], ps_tok[0:TS, 2, k * P:(k + 1) * P], ident[0:TS, 0:TS])
            fill_done("pTs", last)

            pe.wait_ge(s["ba_loaded"], 16 * 2)
            pe.wait_ge(s["aT_ready"], 1)
            for name, o in (("beta", 0), ("a", H)):
                b = to_fill(pe, name)
                for k in range(KD):
                    last = mm(b[0:H, 0:T], wba[:, k, o:o + H], aT[:, k, :], start=k == 0, stop=k == KD - 1)
                fill_done(name, last)
            pe.wait_ge(s["gT_ready"], 1)
            wait_drained(pe, "beta")
            b = to_fill(pe, "gbt")
            for i, src in enumerate((gT, gT, betaT, betaT)):
                last = tr(b[:, i * H:(i + 1) * H], chunk(src, i % 2), ident[0:H, 0:H])
            fill_done("gbt", last)
            wait_drained(pe, "gbt")
            b = to_fill(pe, "gct")
            for i in range(4):
                last = mm(b[:, i * H:(i + 1) * H], (causal if i < 2 else ones)[:], gbt[:, i % 2, :], start=True, stop=True)
            fill_done("gct", last)
            b = to_fill(pe, "gcf")
            for c in range(2):
                last = mm(b[0:H, c * CHUNK:(c + 1) * CHUNK], gbt[:, c, :], causal[:], start=True, stop=True)
            fill_done("gcf", last)

            def products4(name, lhs, rhs):
                b = to_fill(pe, name)
                for i in range(4):
                    last = mm(b[:, i * P:(i + 1) * P], lhs(i), rhs(i), start=True, stop=True)
                fill_done(name, last)

            def transposes4(name, src):
                b = to_fill(pe, name)
                for i in range(4):
                    last = tr(b[:, i * P:(i + 1) * P], src(i), ident[:])
                fill_done(name, last)

            def gdn_step(g, step):
                def name(x):
                    return f"{x}.{g}"

                if step == "norm":
                    pe.wait_ge(s["nsq"], g + 1)
                    for i in range(4):
                        b = to_fill(pe, name(f"n{i}"))
                        fill_done(name(f"n{i}"), mm(b[:, 0:T], ones[:], nsq[:, i, :], start=True, stop=True))
                elif step == "bcast":
                    pe.wait_ge(s["gcF_ready"], 1)
                    wait_drained(pe, "gcf")
                    wait_drained(pe, "beta")
                    for j in range(2):
                        for x, src in (("bcg", gcF), ("bcb", betaT)):
                            b = to_fill(pe, name(f"{x}{j}"))
                            fill_done(name(f"{x}{j}"), mm(b[:, 0:T], sel8[:, 2 * g + j, :], src, start=True, stop=True))
                elif step == "scores":
                    pe.wait_ge(s["nrm"], 2 * (g + 1))
                    pe.wait_ge(s["kb_ready"], 2 * (g + 1))
                    products4(name("AT"), lambda i: chunk(k_of(g, i // 2), i % 2), lambda i: chunk(kb[:, i // 2, :], i % 2))
                    products4(name("QK"), lambda i: chunk(k_of(g, i // 2), i % 2), lambda i: chunk(q_of(g, i // 2), i % 2))
                elif step == "tokens":
                    transposes4(name("kt"), lambda i: chunk(k_of(g, i // 2), i % 2))
                    transposes4(name("vt"), lambda i: chunk(v_of(g, i // 2), i % 2))
                    pe.wait_ge(s["DT0_ready"], g + 1)
                    transposes4(name("T1"), lambda i: DT[:, i, :])
                elif step[:2] == "ad":
                    lv = len(LEVELS) if step == "adl" else int(step[2])
                    wait_drained(pe, name(f"dm{lv - 1}" if lv else "T1"))
                    wait_drained(pe, name("AT"))
                    products4(name(step), lambda i: AT[:, i, :], lambda i: Dm[:, i, :])
                elif step[:2] == "dm":
                    lv = int(step[2])
                    wait_drained(pe, name(f"ad{lv}"))
                    if lv:
                        wait_drained(pe, name(f"tr{lv - 1}"))
                    products4(name(step), lambda i: DT[:, i, :], lambda i: M[:, i, :])
                elif step[:2] == "tr":
                    wait_drained(pe, name(f"dm{step[2]}"))
                    transposes4(name(step), lambda i: Dm[:, i, :])
                elif step == "lt":
                    wait_drained(pe, name("adl"))
                    wait_drained(pe, name(f"tr{len(LEVELS) - 1}"))
                    products4(name("lt"), lambda i: M[:, i, :], lambda i: DT[:, i, :])
                elif step in ("vn0", "vn1"):
                    c = int(step[2])
                    wait_drained(pe, name("lt"))
                    wait_drained(pe, name("kt"))
                    wait_drained(pe, name("vt"))
                    if c:
                        wait_drained(pe, name("ks"))
                    b = to_fill(pe, name(step))
                    for j in range(2):
                        last = mm(b[:, j * P:(j + 1) * P], DT[:, 2 * j + c, :], vb[:, 2 * j + c, :], start=True, stop=True)
                    fill_done(name(step), last)
                elif step in ("s1", "s2"):
                    c = int(step[1]) - 1
                    wait_drained(pe, name(f"vn{c}"))
                    b = to_fill(pe, name(step))
                    for j in range(2):
                        last = mm(b[:, j * P:(j + 1) * P], kd[:, 2 * j + c, :], vn[:, 2 * j + c, :], start=True, stop=True)
                    fill_done(name(step), last)
                elif step == "ks":
                    wait_drained(pe, name("s1"))
                    pe.wait_ge(s["kbg_ready"], 2 * (g + 1))
                    b = to_fill(pe, name(step))
                    for j in range(2):
                        last = mm(b[:, j * P:(j + 1) * P], chunk(kbg[:, j, :], 1), S1[:, j, :], start=True, stop=True)
                    fill_done(name(step), last)
                elif step == "o":
                    wait_drained(pe, name("QK"))
                    b = to_fill(pe, name(step))
                    for j in range(2):
                        o = 2 * j * P
                        mm(b[:, o:o + P], vn[:, 2 * j, :], QKT[:, 2 * j, :], start=True, stop=True)
                        mm(b[:, o + P:o + 2 * P], S1[:, j, :], chunk(qg[:, j, :], 1), start=True, stop=False)
                        last = mm(b[:, o + P:o + 2 * P], vn[:, 2 * j + 1, :], QKT[:, 2 * j + 1, :], start=False, stop=True)
                    fill_done(name(step), last)
                elif step == "onorm":
                    pe.wait_ge(s["osq_ready"], g + 1)
                    for j in range(2):
                        b = to_fill(pe, name(f"on{j}"))
                        fill_done(name(f"on{j}"), mm(b[:, 0:T], ones[:], osq[:, j, :], start=True, stop=True))
                if step in SAMPLE_STEPS:
                    sample_step(g, *SAMPLE_STEPS[step])

            def sample_step(g, step, j):
                h = 2 * g + j
                if step == "skq":
                    pe.wait_ge(s[f"state_loaded{j}"], 16 * (g + 1))
                    pe.wait_ge(s["kq_ready"], g + 1)
                    b = to_fill(pe, f"skq.{h}")
                    for i in range(TS):
                        mm(b[:, 2 * i:2 * i + 2], st[:, j, i, :], kq[:, j, i, :], start=True, stop=True)
                    fill_done(f"skq.{h}", mm(b[:, 16:24], ones[:], qk_s[:, j, :], start=True, stop=True))
                elif step == "srow":
                    pe.wait_ge(s["svn_ready"], h + 1)
                    b = to_fill(pe, f"srow.{h}")
                    tr(b[0:TS, 0:P], k_of(g, j)[:, TP:T], ident[:])
                    fill_done(f"srow.{h}", tr(b[0:TS, P:2 * P], sv[:, 2, :], ident[:]))
                else:
                    wait_drained(pe, f"srow.{h}")
                    for i in range(2):
                        b = to_fill(pe, f"kv{i}.{h}")
                        fill_done(f"kv{i}.{h}", mm(b[:], krow[:], vbd[:, 4 * i:4 * i + 4, :].rearrange("b i v -> b (i v)"),
                                                   start=True, stop=True))

            for kind, n, x in TIMETABLE:
                if kind == "block" and n < N_BLOCKS:
                    if x == 0:
                        b = to_fill(pe, f"proj{n}")
                        if n % 2 == 0:
                            w = take_chunk(pe, "in", BLOCKS[n][2])
                        o = P * (n % 2)
                    for k in ((0, 1, 2), (3, 4, 5), (6, 7))[x]:
                        last = mm(b[:, 0:T], w[:, k, o:o + P], aT[:, k, :], start=k == 0, stop=k == KD - 1)
                    if x == 2:
                        fill_done(f"proj{n}", last)
                elif kind == "gdn":
                    keep = b
                    gdn_step(n, x)
                    b = keep
                elif kind == "conf_rows":
                    pe.wait_ge(s["u_ready"], 8)
                    bb = to_fill(pe, f"crow{n}")
                    for i in range(CB):
                        if n == 0:
                            last = tr(bb[0:30, i * P:(i + 1) * P], up[:, i, 256:286], ident[:])
                        else:
                            last = tr(bb[0:TS, i * P:(i + 1) * P], us[:, i, :, CK - 1], ident[:])
                    fill_done(f"crow{n}", last)
                elif kind == "tail":
                    wait_drained(pe, f"proj{8 + 22}")
                    wait_drained(pe, f"proj{8 + 23}")
                    bb = to_fill(pe, f"tail{n}")
                    for i in range(4):
                        m = QKV_ORDER.index(divmod(4 * n + i, H))
                        last = tr(bb[0:11, i * P:(i + 1) * P], tail[:, m, :], ident[:])
                    fill_done(f"tail{n}", last)
                elif kind == "conf_mean":
                    pe.wait_ge(s["conf_done"], 1)
                    bb = to_fill(pe, "cmu")
                    for i in range(CB):
                        last = mm(bb[:, 0:T], ones[:], cv[:, i, :], start=i == 0, stop=i == CB - 1)
                    fill_done("cmu", last)
                elif kind == "conf_var":
                    pe.wait_ge(s["csq"], 1)
                    bb = to_fill(pe, "cvar")
                    for i in range(CB):
                        last = mm(bb[:, 0:T], ones[:], conf_sq[:, i, :], start=i == 0, stop=i == CB - 1)
                    fill_done("cvar", last)

            def dense(name, kind, per, n_k, rhs):
                for i in range(KD):
                    w = take_chunk(pe, kind, i // per)
                    b = to_fill(pe, f"{name}{i}")
                    o = P * (i % per)
                    for k in range(n_k):
                        last = mm(b[:, 0:T], w[:, k, o:o + P], rhs(k), start=k == 0, stop=k == n_k - 1)
                    fill_done(f"{name}{i}", last)

            pe.wait_ge(s["cv_ready"], 1)
            dense("bb", "conf", 4, CB, lambda k: cv[:, k, :])
            pe.wait_ge(s["onorm_ready"], 5)
            dense("ba", "gdn", 2, H, lambda k: oT[:, k, :])
            pe.wait_ge(s["mix"], KD)
            dense("wo", "out", 2, KD, lambda k: aT[:, k, :])

            sum_squares("rms2", 2)
            pe.wait_ge(s["aT_ready"], 2)
            b = to_fill(pe, "logits")
            for j in range(NTB):
                for k in range(KD):
                    last = mm(b[0:TB, j * NE:(j + 1) * NE], aT[:, k, j * TB:(j + 1) * TB], wr[:, k, :],
                              start=k == 0, stop=k == KD - 1)
            fill_done("logits", last)
            for i in range(6):
                b = to_fill(pe, f"hm{i}")
                for m in range(4):
                    k = 4 * (i % 2) + m
                    last = tr(b[0:TB, m * P:(m + 1) * P], aT[:, k, (i // 2) * TB:(i // 2 + 1) * TB], ident[:])
                fill_done(f"hm{i}", last)
            pe.wait_ge(s["gates"], 1)
            b = to_fill(pe, "gTr")
            for j in range(NTB):
                last = tr(b[0:NE, j * TB:(j + 1) * TB], gates[:, j, :], ident[0:TB, 0:TB])
            fill_done("gTr", last)
            pe.wait_ge(s["consts"], CONSTS + 2)
            b = to_fill(pe, "rank")
            for j in range(NTB):
                for i in range(j + 1):
                    w = before[:] if i == j else ones[0:TB, 0:TB]
                    mm(b[0:TB, j * NE:(j + 1) * NE], w, sel[:, i, :], start=i == 0, stop=i == j)
            for i in range(NTB):
                last = mm(b[:, NTB * NE:(NTB + 1) * NE], ones[0:TB, :], sel[:, i, :], start=i == 0, stop=i == NTB - 1)
            fill_done("rank", last)
            pe.wait_ge(s["bd_loaded"], 16)
            wait_drained(pe, "gTr")
            for i in range(KD):
                b = to_fill(pe, f"bd{i}")
                fill_done(f"bd{i}", mm(b[:, 0:T], b_down[0:NE, i * P:(i + 1) * P], gatesT[:], start=True, stop=True))
            for i in range(8):
                pe.wait_ge(drained[i], before_experts[i])

            aux = [bank[6], bank[7]]
            half = 4 * CAP

            def gather(sm, n):
                pe.wait_ge(sm["onehot"], n + 1)
                for h in range(2):
                    for i in range(4):
                        k = 4 * h + i
                        for j in range(NTB):
                            last = mm(aux[h][:, i * CAP:(i + 1) * CAP], hm_tok[0:TB, j, k * P:(k + 1) * P],
                                      onehot[:, j, :], start=j == 0, stop=j == NTB - 1)
                    last.then_inc(sm["gather_filled"], 1)
                    if h == 0:
                        yield

            def expert(sm, sems, n, fills, base, first, last_one):
                pe.wait_ge(sm["xsel"], n * 2 + 2)
                for c in range(KD):
                    pe.wait_ge(sems[c], fills(c))
                    for f in range(16):
                        o = (f % 4) * CAP
                        last = mm(bank[f // 4][:, o:o + CAP], ring[:, c, f * P:(f + 1) * P], xsel[:, c, :],
                                  start=c == 0 and f % 4 == 0, stop=c == KD - 1, skip_group_check=True)
                    last.then_inc(sm["chunk_used"], 1)
                if not last_one:
                    if not first:
                        pe.wait_ge(sm["pt_filled"], n)
                        pe.wait_ge(sm["pgT"], n)
                        pe.wait_ge(sm["sc_added"], n * 8 - 8)
                    for _ in gather(sm, n + 1):
                        pass
                if not first:
                    scatter(sm, n - 1, not last_one)
                pe.wait_ge(sm["gated"], n + 1)
                if first:
                    pe.wait_ge(sm["xsel"], n * 2 + 3)
                else:
                    pe.wait_ge(sm["sc_added"], n * 8 - 1)
                for j in range(NTB):
                    last = tr(aux[0][0:CAP, j * TB:(j + 1) * TB], gated[:, j, :], ident[0:TB, 0:TB])
                last.then_inc(sm["pt_filled"], 1)
                pe.wait_ge(sm["hid"], n + 1)
                if not first:
                    pe.wait_ge(sm["yT"], n * 2)
                for c in range(KD // 2):
                    pe.wait_ge(sems[KD + c], fills(KD + c))
                    w = chunk_view("down", KD + c)
                    for k in range(2):
                        for i in range(KD):
                            o = (i % 4) * CAP
                            last = mm(bank[4 + i // 4][:, o:o + CAP], w[:, k, i * P:(i + 1) * P], gbuf[:, 2 * c + k, :],
                                      start=c == 0 and k == 0 and i % 4 == 0, stop=c == KD // 2 - 1 and k == 1,
                                      skip_group_check=True)
                    last.then_inc(sm["chunk_used"], 1)

            def scatter(sm, n, gathered):
                pe.wait_ge(sm["yT"], n * 2 + 2)
                for h in range(2):
                    if gathered:
                        pe.wait_ge(sm["xsel"], n * 2 + 4 + h + 1)
                    elif h == 0:
                        pe.wait_ge(sm["pgT"], n + 1)
                    else:
                        pe.wait_ge(sm["sc_added"], n * 8)
                    for i in range(4):
                        last = tr(aux[h][0:CAP, i * P:(i + 1) * P], yT[:, 4 * h + i, :], ident[:])
                    last.then_inc(sm["yt_filled"], 1)
                pe.wait_ge(sm["ysb"], n * 2 + 2)
                pe.wait_ge(sm["pgT"], n + 1)
                for i in range(KD):
                    if i >= 2:
                        pe.wait_ge(sm["sc_added"], n * 8 + i - 1)
                    mm(aux[i % 2][:, 0:T], ysb[:, i * P:(i + 1) * P], pgT, start=True, stop=True).then_inc(sm["sc_filled"], 1)

            def run_experts(sm, sems, base, fills):
                for _ in gather(sm, base):
                    pass
                expert(sm, sems, base, lambda c: fills(c, 0), base, True, False)
                with pe.Fori(1, NE - 1) as e:
                    expert(sm, sems, base + e, lambda c: fills(c, e), base, False, False)
                expert(sm, sems, base + NE - 1, lambda c: fills(c, NE - 1), base, False, True)
                scatter(sm, base + NE - 1, False)

            run_experts(first, loaded, 0, lambda c, e: e * 16 + 16 * (slot_fills[c] + 1))
            most = pe.value_load(flag[0:1, 0:1], min_val=0, max_val=T)
            with pe.If(most > CAP):
                pe.wait_ge(first["sc_added"], 8 * NE)
                with pe.Fori(1, PASSES) as j:
                    pe.wait_ge(more["sc_added"], (j - 1) * (8 * NE))
                    run_experts(more, more_loaded, (j - 1) * NE, lambda c, e: (j - 1) * (16 * NE) + (e * 16 + 16))

            sum_squares("rms3", 3)
            pe.wait_ge(s["aT_ready"], 3)
            pe.wait_ge(s["late_loaded"], 16 * 5)
            wp = chunk_view("down", 4)
            for i in range(KD):
                b = to_fill(pe, f"pg{i}")
                w = chunk_view("in", i // 2)
                for k in range(KD):
                    last = mm(b[:, 0:T], w[:, k, P * (i % 2):P * (i % 2) + P], aT[:, k, :], start=k == 0, stop=k == KD - 1)
                fill_done(f"pg{i}", last)
                b = to_fill(pe, f"pp{i}")
                for k in range(2):
                    last = mm(b[:, 0:T], wp[:, k, i * P:(i + 1) * P], pT[:, k, :], start=k == 0, stop=k == 1)
                fill_done(f"pp{i}", last)
            sum_squares("rms4", 4)
            pe.wait_ge(s["aT_ready"], 4)
            for t in range(3):
                w = P if t < 2 else TS
                for h in range(2):
                    b = to_fill(pe, f"y{t}{h}")
                    for i in range(4):
                        last = tr(b[0:w, i * P:(i + 1) * P], aT[:, 4 * h + i, t * P:t * P + w], ident[:])
                    fill_done(f"y{t}{h}", last)

        @block.scalar
        def _(act):
            tell = Teller(act, s, "act_order")
            A = nc.scalar.activation

            def out_of(instruction, name):
                instruction.then_inc(drain_sem(name), 1)
                wait_drained(act, name)

            def load(dst, src, name):
                act.dma_start(dst, src).then_inc(s[name], 16)

            xp, xsm = a["x_prompt"][0], a["x_sample"].rearrange("b s d -> (b s) d")
            for t in range(2):
                load(xs[:, t, :], xp[t * P:(t + 1) * P, :], "x_loaded")
            load(xs[0:TS, 2, :], xsm, "x_loaded")
            for name, r, n in (("norm_mix", 0, 8), ("norm_ffn", 8, 8), ("norm_ple", 16, 8), ("norm_final", 24, 8),
                               ("conf_dw_b", 32, 4), ("conf_ln_g", 36, 4), ("conf_ln_b", 40, 4), ("gdn_norm", 44, 1)):
                v = a[name] if name == "norm_final" else a[name][0]
                load(stage[r:r + n, 0, :], v.rearrange("(r c) -> r c", c=P), "params_loaded")
            load(stage[0:96, 1, :], a["conv_qkv_w"][0].rearrange("t (r c) -> (t r) c", c=P), "params_loaded")
            load(stage[0:CK * CB, 2, :], a["conf_dw_w"][0].rearrange("t (r c) -> (t r) c", c=P), "params_loaded")
            load(small8[:, 0:1], a["a_log"].rearrange("o h -> h o"), "params_loaded")
            load(small8[:, 1:2], a["dt_bias"].rearrange("o h -> h o"), "params_loaded")
            load(brt[:], a["b_router"][0:1, :].broadcast_to([TB, NE]), "params_loaded")
            load(hist_rows, a["state_qkv_conv"][0].rearrange("b i c -> (b i) c"), "rows_loaded")
            load(bgu_rows, a["b_gate_up"][0], "rows_loaded")
            cs = a["state_conf_conv"][0].rearrange("b i c -> (b i) c")
            for i in range(2):
                load(conf_rows[0:120, i, :], cs[120 * i:120 * (i + 1), :], "rows_loaded")
            for t in range(2):
                load(ps_tok[:, t, :], a["p_prompt"][0, 0, t * P:(t + 1) * P, :], "rows_loaded")
            load(ps_tok[0:TS, 2, :], a["p_sample"][0].rearrange("b s c -> (b s) c"), "rows_loaded")
            state_in = a["state_gdn"][0].rearrange("b h k v -> h k b v")
            state_out = out[5][0].rearrange("b h k v -> h k b v")
            for j in range(2):
                load(st[:, j, :, :], state_in[j], f"state_loaded{j}")
            act.dma_start(out[6][0, :, 0:HIST - 1, :], a["state_qkv_conv"][0, :, 1:HIST, :]).then_inc(s["outs"], 16)
            act.dma_start(out[7][0, :, 0:CK - 2, :], a["state_conf_conv"][0, :, 1:CK - 1, :]).then_inc(s["outs"], 16)

            out_of(nc.scalar.copy(par[:], to_drain(act, "par0")[:, 0:45]), "par0")
            b = to_drain(act, "par1")
            for t in range(4):
                i = nc.scalar.copy(wconv[:, t, :].rearrange("p (g k j) -> p k g j", g=4, k=3),
                                   b[:, 24 * t:24 * (t + 1)].rearrange("p (k g j) -> p k g j", k=3, g=4))
                if t == 3:
                    out_of(i, "par1")
            out_of(nc.scalar.copy(wdw[:].rearrange("p t b -> p (t b)"), to_drain(act, "par2")[:, 0:CK * CB]), "par2")
            for t in range(3):
                w = P if t < 2 else TS
                b = to_drain(act, f"x{t}0")
                out_of(nc.scalar.copy(xT[:, 0:4, t * P:t * P + w], b[:, 0:4 * w].rearrange("p (k t) -> p k t", k=4)), f"x{t}0")

            def squares(names):
                for x in names:
                    wait_drained(act, x)
                tell(A(aT[:], xT[:], ACT.Square), "squares")

            def root(dst, name, scale, e=0):
                act.wait_ge(s["consts"], CONSTS)
                b = to_drain(act, name)
                out_of(A(dst, b[:, 0:T], ACT.Sqrt, bias=eps[:, e:e + 1], scale=scale), name)

            squares([f"x{t}1" for t in range(3)])
            root(rstd[:], "rms1", 1.0 / D)
            out_of(nc.scalar.copy(bguT[:].rearrange("p f e -> p (f e)"), to_drain(act, "bgu")), "bgu")
            out_of(nc.scalar.copy(pT[:, :, 0:TP], to_drain(act, "pT")[:].rearrange("p (k t) -> p k t", k=2)), "pT")
            out_of(nc.scalar.copy(pT[:, :, TP:T], to_drain(act, "pTs")[:, 0:2 * TS].rearrange("p (k t) -> p k t", k=2)), "pTs")
            out_of(A(betaT, to_drain(act, "beta")[0:H, 0:T], ACT.Sigmoid), "beta")
            act.wait_ge(s["params_loaded"], 16 * PARAM_DMAS)
            tell(A(small8[:, 2:3], small8[:, 0:1], ACT.Exp), "expa")
            act.wait_ge(s["sp_in"], 1)
            tell(A(tmp8b, tmp8b, ACT.Exp), "e1_ready")
            act.wait_ge(s["gates_in"], 1)
            tell(A(tmp8b, tmp8b, ACT.Ln), "ln_ready")
            out_of(nc.scalar.copy(gbt[:].rearrange("p i h -> p (i h)"), to_drain(act, "gbt")[:, 0:4 * H]), "gbt")
            act.wait_ge(s["esc_in"], 1)
            tell(A(esc[:], esc[:], ACT.Exp), "esc_ready")

            def gdn_step(g, step):
                def name(x):
                    return f"{x}.{g}"

                if step == "norm" and g:
                    for j in range(2):
                        act.wait_ge(s[f"state_stored{j}"], 16 * g)
                        load(st[:, j, :, :], state_in[2 * g + j], f"state_loaded{j}")
                if step == "norm":
                    for i in range(4):
                        root(nstd[:, i, :], name(f"n{i}"), 1.0)
                elif step == "onorm":
                    for j in range(2):
                        root(ostd[:, j, :], name(f"on{j}"), 1.0 / P)
                elif step == "bcast":
                    if g:
                        act.wait_ge(s["sscaled"], 2 * g)
                        act.wait_ge(s["os_ready"], 2 * g)
                        act.wait_ge(s["kbg_ready"], 2 * g)
                    for j in range(2):
                        b = to_drain(act, name(f"bcg{j}"))
                        act.wait_ge(s["dec_diff"], 4 * g + 2 * j + 2)
                        out_of(A(eg[:, j, :], b[:, 0:T], ACT.Exp), name(f"bcg{j}"))
                    tell(A(dec[:], dec[:], ACT.Exp), "dec_exp")
                elif step == "tokens":
                    out_of(nc.scalar.copy(Dm[:].rearrange("p i c -> p (i c)"), to_drain(act, name("T1"))), name("T1"))
                elif step[:2] == "tr":
                    out_of(nc.scalar.copy(DT[:].rearrange("p i c -> p (i c)"), to_drain(act, name(step))), name(step))
                elif step in ("vn0", "vn1"):
                    c = int(step[2])
                    b = to_drain(act, name(step))
                    out_of(nc.scalar.copy(vn[:, c:4:2, :], b[:, 0:2 * P].rearrange("p (j v) -> p j v", j=2)), name(step))
                elif step == "s1":
                    b = to_drain(act, name(step))
                    out_of(nc.scalar.copy(S1[:], b[:, 0:2 * P].rearrange("p (j v) -> p j v", j=2)), name(step))
                elif step == "o":
                    b = to_drain(act, name(step))
                    out_of(nc.scalar.copy(oT[:, 2 * g:2 * g + 2, 0:TP], b[:].rearrange("p (j t) -> p j t", j=2)), name(step))
                    wait_drained(act, name("s2"))
                    act.dma_start(out[2][0, 0, 2 * g:2 * g + 2].rearrange("j k v -> k j v"), sfin[:]).then_inc(s["sfin_stored"], 16)
                j = {"tr2": 0, "lt": 1}.get(step)
                if j is not None:
                    h = 2 * g + j
                    wait_drained(act, f"kv0.{h}")
                    wait_drained(act, f"kv1.{h}")
                    act.dma_start(state_out[h], st[:, j, :, :]).then_inc(s[f"state_stored{j}"], 16)

            n_rows = 0
            for kind, n, x in TIMETABLE:
                if kind == "block" and 1 <= n:
                    what, i, _ = BLOCKS[n - 1]
                    name = f"proj{n - 1}"
                    if x == 0:
                        b = to_drain(act, name)
                        if what == "val":
                            if i >= 2:
                                act.wait_ge(s["u_ready"], 2 * (i - 1))
                            out_of(nc.scalar.copy(vals[i % 2], b[:, 0:T]), name)
                        elif what == "sig":
                            if i:
                                act.wait_ge(s["u_ready"], 2 * i)
                            out_of(A(sig, b[:, 0:T], ACT.Sigmoid), name)
                        elif what == "qkv":
                            if i:
                                act.wait_ge(s["conv_ready"], i)
                            else:
                                act.wait_ge(s["consts"], CONSTS)
                            tell(nc.scalar.copy(raw[:, HIST:HIST + TP], b[:, 0:TP]))
                            out_of(nc.scalar.copy(tail[:, i, :], b[:, TP - HIST:T]), name)
                        elif what == "z":
                            if i:
                                wait_drained(act, f"proj{n - 2}")
                            else:
                                act.wait_ge(s["qkv_ready"], 24)
                            tell(A(sig, b[:, 0:T], ACT.Sigmoid), "z_sig")
                        else:
                            dst = gaT if what == "ga" else gbT
                            out_of(A(dst[:, i, :], b[:, 0:T], ACT.Sigmoid), name)
                    elif x == 1 and what == "qkv":
                        act.wait_ge(s["conv_ready"], i + 1)
                        if i == 0:
                            act.wait_ge(s["u_ready"], 8)
                        tell(A(sig[:, 0:TP], acc[:, 0:TP], ACT.Sigmoid), "silu_sig")
                        if i % 6 == 5:
                            act.wait_ge(s["sample_acc"], i // 6 + 1)
                            tell(A(stmp[:], sacc[:], ACT.Sigmoid), "sample_sig")
                elif kind == "gdn":
                    gdn_step(n, x)
                elif kind in ("conf_rows", "tail"):
                    name = f"crow{n}" if kind == "conf_rows" else f"tail{n}"
                    rows = (30 if n == 0 else TS) if kind == "conf_rows" else 11
                    b = to_drain(act, name)
                    if n_rows:
                        act.wait_ge(s["tail_stored"], 16 * n_rows)
                    out_of(nc.scalar.copy(qrow[0:rows, :], b[0:rows, :]), name)
                    c0 = 512 * n
                    if kind == "tail":
                        act.dma_start(out[3][0, 0, :, c0:c0 + 512], qrow[0:HIST, :]).then_inc(s["tail_stored"], 16)
                        act.dma_start(out[6][0, :, HIST - 1, c0:c0 + 512], qrow[HIST:11, :]).then_inc(s["tail_stored"], 16)
                        n_rows += 2
                    elif n == 0:
                        act.dma_start(out[4][0, 0], qrow[0:30, :]).then_inc(s["tail_stored"], 16)
                        n_rows += 1
                    else:
                        act.dma_start(out[7][0, :, CK - 2, :], qrow[0:TS, :]).then_inc(s["tail_stored"], 16)
                        n_rows += 1
                elif kind == "conf_var":
                    root(vals[1], "cvar", 1.0 / CC, 1)
                    act.wait_ge(s["caff"], 1)
                    tell(A(conf_sq, cv[:], ACT.Sigmoid), "csig")

            act.wait_ge(s["cv_ready"], 1)
            act.dma_start(b_down[0:NE, :], a["b_down"][0]).then_inc(s["bd_loaded"], 16)
            squares([f"wo{i}" for i in range(KD)])
            root(rstd[:], "rms2", 1.0 / D)
            for i in range(6):
                b = to_drain(act, f"hm{i}")
                out_of(nc.scalar.copy(hm_tok[0:TB, i // 2, (i % 2) * 512:(i % 2 + 1) * 512], b[0:TB, :]), f"hm{i}")
            act.wait_ge(s["nmax"], 1)
            for j in range(NTB):
                tell(A(gates[:, j, :], lg[:, j, 0:NE], ACT.Exp, bias=nmax[:, j:j + 1]), "wexp")
            out_of(nc.scalar.copy(gatesT, to_drain(act, "gTr")[0:NE, 0:T]), "gTr")

            aux = [bank[6], bank[7]]
            half = 4 * CAP

            def four(v, h):
                return v[:, 4 * h:4 * h + 4, :].rearrange("p k c -> p (k c)")

            def gathered(sm, n):
                for h in range(2):
                    act.wait_ge(sm["gather_filled"], n * 2 + h + 1)
                    nc.scalar.copy(four(xsel, h), aux[h][:, 0:half]).then_inc(sm["xsel"], 1)

            def expert(sm, n, first, last_one):
                act.wait_ge(sm["gate_in"], n + 1)
                A(sbuf_sig[:], gbuf[:], ACT.Sigmoid, scale=ALPHA).then_inc(sm["gate_sig"], 1)
                if not last_one:
                    gathered(sm, n + 1)
                if not first:
                    slot_rows(sm, n - 1)
                act.wait_ge(sm["pt_filled"], n + 1)
                nc.scalar.copy(pgT, aux[0][0:CAP, 0:T]).then_inc(sm["pgT"], 1)
                act.wait_ge(sm["chunk_used"], n * RING_E + RING_E)
                for h in range(2):
                    nc.scalar.copy(four(yT, h), bank[4 + h][:, 0:half]).then_inc(sm["yT"], 1)

            def slot_rows(sm, n):
                for h in range(2):
                    act.wait_ge(sm["yt_filled"], n * 2 + h + 1)
                    nc.scalar.copy(ysb[:, 512 * h:512 * (h + 1)], aux[h][0:CAP, :]).then_inc(sm["ysb"], 1)

            def run_experts(sm, base):
                gathered(sm, base)
                expert(sm, base, True, False)
                with act.Fori(1, NE - 1) as e:
                    expert(sm, base + e, False, False)
                expert(sm, base + NE - 1, False, True)
                slot_rows(sm, base + NE - 1)

            run_experts(first, 0)
            most = act.value_load(flag[0:1, 0:1], min_val=0, max_val=T)
            with act.If(most > CAP):
                with act.Fori(1, PASSES) as j:
                    run_experts(more, (j - 1) * NE)
                act.wait_ge(more["sc_added"], (PASSES - 1) * NE * KD)

            act.wait_ge(first["sc_added"], NE * KD)
            tell(A(aT[:], xT[:], ACT.Square), "squares")
            root(rstd[:], "rms3", 1.0 / D)
            for i in range(KD):
                b = to_drain(act, f"pg{i}")
                if i >= 2:
                    act.wait_ge(s["x3"], i - 1)
                out_of(A(pieces[:, i % 2, :], b[:, 0:T], ACT.Sigmoid), f"pg{i}")
            act.wait_ge(s["x3"], KD)
            tell(A(aT[:], xT[:], ACT.Square), "squares")
            root(rstd[:], "rms4", 1.0 / D)
            for t in range(3):
                w = P if t < 2 else TS
                for h in range(2):
                    name = f"y{t}{h}"
                    b = to_drain(act, name)
                    out_of(nc.scalar.copy(yrows[0:w, t, 512 * h:512 * (h + 1)], b[0:w, :]), name)
                    dst = out[0][0, t * P:(t + 1) * P, :] if t < 2 else out[1].rearrange("b s d -> (b s) d")
                    act.dma_start(dst[:, 512 * h:512 * (h + 1)], yrows[0:w, t, 512 * h:512 * (h + 1)]).then_inc(s["outs"], 16)
            act.wait_ge(s["outs"], 16 * 8)
            act.wait_ge(s["tail_stored"], 16 * n_rows)
            act.wait_ge(s["sfin_stored"], 16 * 4)
            for j in range(2):
                act.wait_ge(s[f"state_stored{j}"], 16 * 4)

        @block.vector
        def _(dve):
            v = nc.vector
            tell = Teller(dve, s, "dve_order")

            def out_of(instruction, name):
                instruction.then_inc(drain_sem(name), 1)
                wait_drained(dve, name)

            for t in range(3):
                w = P if t < 2 else TS
                b = to_drain(dve, f"x{t}1")
                out_of(v.tensor_copy(xT[:, 4:8, t * P:t * P + w], b[:, 0:4 * w].rearrange("p (k t) -> p k t", k=4)), f"x{t}1")

            def norm(name, gain):
                wait_drained(dve, name)
                tell(v.reciprocal(rstd[:], rstd[:]))
                for k in range(KD):
                    i = v.scalar_tensor_tensor(aT[:, k, :], xT[:, k, :], par[:, gain + k:gain + k + 1], rstd[:], ALU.mult, ALU.mult)
                    tell(i, "aT_ready" if k == KD - 1 else None)

            wait_drained(dve, "par0")
            norm("rms1", 0)
            for i in range(2):
                b = to_drain(dve, f"hist{i}")
                n = 12 * TS * HIST
                out_of(v.tensor_copy(hist[:, 12 * i:12 * (i + 1), :].rearrange("p m r -> p (m r)"), b[:, 0:n]), f"hist{i}")
            for i in range(2):
                b = to_drain(dve, f"ch{i}")
                for m in range(CB):
                    c = v.tensor_copy(us[:, m, 4 * i:4 * i + 4, 0:CK - 1], b[:, 120 * m:120 * (m + 1)].rearrange("p (b t) -> p b t", b=4))
                    if m == CB - 1:
                        out_of(c, f"ch{i}")
            b = to_drain(dve, "a")
            dve.wait_ge(s["params_loaded"], 16 * PARAM_DMAS)
            out_of(v.tensor_scalar(tmp8, b[0:H, 0:T], small8[:, 1:2], None, ALU.add), "a")
            tell(v.tensor_scalar(tmp8b, tmp8, -1.0, None, ALU.mult))
            tell(v.tensor_tensor(tmp8b, tmp8b, tmp8, ALU.min), "sp_in")
            dve.wait_ge(s["e1_ready"], 1)
            tell(v.tensor_scalar(tmp8b, tmp8b, 1.0, None, ALU.add), "gates_in")
            dve.wait_ge(s["ln_ready"], 1)
            tell(v.scalar_tensor_tensor(tmp8, tmp8, 0.0, tmp8b, ALU.max, ALU.add))
            dve.wait_ge(s["expa"], 1)
            tell(v.tensor_scalar(gT, tmp8, small8[:, 2:3], -1.0, ALU.mult, ALU.mult), "gT_ready")
            tell(v.tensor_copy(gcF[:, TP:T], gT[:, TP:T]), "gcF_ready")
            b = to_drain(dve, "gct")
            out_of(v.tensor_copy(gct[:].rearrange("p i h -> p (i h)"), b[:, 0:4 * H]), "gct")
            tell(v.tensor_tensor(esc[:, 0:2, :], gct[:, 2:4, :], gct[:, 0:2, :], ALU.subtract))
            tell(v.tensor_copy(esc[:, 2:4, :], gct[:, 2:4, :]), "esc_in")
            b = to_drain(dve, "gcf")
            out_of(v.tensor_copy(gcF[:, 0:TP], b[0:H, 0:TP]), "gcf")

            def four(x):
                return x[:].rearrange("p i c -> p (i c)")

            def bank4(b):
                return b[:].rearrange("p (i c) -> p i c", i=4)

            def each4(x):
                return x.unsqueeze(1).broadcast_to([P, 4, P])

            def gdn_step(g, step):
                def name(x):
                    return f"{x}.{g}"

                q2, k2 = qkvT[:, 6 * g:6 * g + 2, :], qkvT[:, 6 * g + 2:6 * g + 4, :]
                if step == "norm":
                    if g:
                        wait_drained(dve, f"o.{g - 1}")
                    for i in range(4):
                        wait_drained(dve, name(f"n{i}"))
                    tell(v.reciprocal(nstd[:], nstd[:]))
                    tell(v.scalar_tensor_tensor(q2, q2, float(P) ** -0.5, nstd[:, 0:2, :], ALU.mult, ALU.mult), "nrm")
                    tell(v.tensor_tensor(k2, k2, nstd[:, 2:4, :], ALU.mult), "nrm")
                    tell(v.tensor_copy(kq[:, :, :, 0], k2[:, :, TP:T]))
                    tell(v.tensor_copy(kq[:, :, :, 1], q2[:, :, TP:T]))
                    tell(v.tensor_tensor(qk_s[:], k2[:, :, TP:T], q2[:, :, TP:T], ALU.mult), "kq_ready")
                elif step == "bcast":
                    for j in range(2):
                        h = 2 * g + j
                        b = to_drain(dve, name(f"bcg{j}"))
                        for c in range(2):
                            tell(v.tensor_scalar(dec[:, 2 * j + c, :], chunk(b, c), gct[:, c, h:h + 1], 0.0,
                                                 ALU.subtract, ALU.min), "dec_diff")
                        b = to_drain(dve, name(f"bcb{j}"))
                        tell(v.tensor_tensor(kb[:, j, :], k_of(g, j), b[:, 0:T], ALU.mult), "kb_ready")
                        out_of(v.tensor_copy(beta_s[:, j, :], b[:, TP:T]), name(f"bcb{j}"))
                    dve.wait_ge(s["dec_exp"], g + 1)
                    tell(v.tensor_tensor(dec[:], dec[:], each4(causal[:]), ALU.mult))
                elif step == "scores":
                    b = to_drain(dve, name("AT"))
                    out_of(v.tensor_tensor(four(AT), b[:], four(dec), ALU.mult), name("AT"))
                    dve.wait_ge(s["masks_ready"], 1)
                    b = to_drain(dve, name("QK"))
                    out_of(v.tensor_tensor(four(QKT), b[:], four(dec), ALU.mult), name("QK"))
                    tell(v.tensor_tensor(DT[:], AT[:], each4(neg_first[:]), ALU.mult))
                    tell(v.tensor_tensor(DT[:], DT[:], each4(ident[:]), ALU.add), "DT0_ready")
                elif step == "tokens":
                    dve.wait_ge(s["esc_ready"], 1)
                    wait_drained(dve, "gbt")
                    for job, dst, col in (("kt", kd, esc[:, 0:2, :]), ("vt", vb, gbt[:, 2:4, :])):
                        b = to_drain(dve, name(job))
                        for i in range(4):
                            h = 2 * g + i // 2
                            x = v.tensor_scalar(dst[:, i, :], b[:, i * P:(i + 1) * P], col[:, i % 2, h:h + 1], None, ALU.mult)
                            if i == 3:
                                out_of(x, name(job))
                            else:
                                tell(x)
                elif step[:2] == "ad":
                    lv = len(LEVELS) if step == "adl" else int(step[2])
                    b = to_drain(dve, name(step))
                    out_of(v.tensor_tensor(M[:], bank4(b), each4(neg_mask[:, lv, :]), ALU.mult), name(step))
                elif step[:2] == "dm":
                    b = to_drain(dve, name(step))
                    out_of(v.tensor_tensor(four(Dm), four(Dm), b[:], ALU.add), name(step))
                elif step == "lt":
                    b = to_drain(dve, name(step))
                    out_of(v.tensor_tensor(four(DT), four(DT), b[:], ALU.add), name(step))
                elif step == "ks":
                    b = to_drain(dve, name(step))
                    out_of(v.tensor_tensor(vb[:, 1:4:2, :], vb[:, 1:4:2, :], b[:, 0:2 * P].rearrange("p (j v) -> p j v", j=2),
                                           ALU.subtract), name(step))
                elif step == "s2":
                    b = to_drain(dve, name(step))
                    if g:
                        dve.wait_ge(s["sfin_stored"], 16 * g)
                    for j in range(2):
                        h = 2 * g + j
                        x = v.scalar_tensor_tensor(sfin[:, j, :], S1[:, j, :], esc[:, 3, h:h + 1], b[:, j * P:(j + 1) * P],
                                                   ALU.mult, ALU.add)
                        if j:
                            out_of(x, name(step))
                        else:
                            tell(x)
                elif step == "onorm":
                    for j in range(2):
                        wait_drained(dve, name(f"on{j}"))
                    tell(v.reciprocal(ostd[:], ostd[:]))
                    o2 = oT[:, 2 * g:2 * g + 2, :]
                    tell(v.scalar_tensor_tensor(o2, o2, par[:, 44:45], ostd[:], ALU.mult, ALU.mult), "onorm_ready")
                if step in SAMPLE_STEPS:
                    sample_step(g, *SAMPLE_STEPS[step])

            def sample_step(g, step, j):
                h = 2 * g + j
                if step == "skq":
                    b = to_drain(dve, f"skq.{h}")
                    wait_drained(dve, f"bcg{j}.{g}")
                    kv = b[:, 0:2 * TS].rearrange("p (i x) -> p i x", x=2)
                    e = eg[:, j, TP:T]
                    tell(v.tensor_tensor(sv[:, 0, :], kv[:, :, 0], e, ALU.mult))
                    tell(v.tensor_tensor(sv[:, 1, :], kv[:, :, 1], e, ALU.mult))
                    out_of(v.tensor_copy(sv[:, 3, :], b[:, 16:24]), f"skq.{h}")
                    tell(v.tensor_tensor(sv[:, 0, :], v_of(g, j)[:, TP:T], sv[:, 0, :], ALU.subtract))
                    tell(v.tensor_tensor(sv[:, 2, :], sv[:, 0, :], beta_s[:, j, :], ALU.mult), "svn_ready")
                    tell(v.tensor_tensor(sv[:, 3, :], sv[:, 3, :], sv[:, 2, :], ALU.mult))
                    tell(v.tensor_tensor(oT[:, h, TP:T], sv[:, 1, :], sv[:, 3, :], ALU.add), "os_ready")
                elif step == "srow":
                    b = to_drain(dve, f"srow.{h}")
                    tell(v.tensor_copy(krow[:], b[0:TS, 0:P]))
                    out_of(v.tensor_tensor(vbd[:], b[0:TS, P:2 * P].unsqueeze(1).broadcast_to([TS, TS, P]),
                                           ident[0:TS, 0:TS].unsqueeze(2).broadcast_to([TS, TS, P]), ALU.mult), f"srow.{h}")
                else:
                    dve.wait_ge(s["sscaled"], h + 1)
                    for i in range(2):
                        b = to_drain(dve, f"kv{i}.{h}")
                        x = st[:, j, 4 * i:4 * i + 4, :]
                        out_of(v.tensor_tensor(x, x, b[:].rearrange("p (i v) -> p i v", i=4), ALU.add), f"kv{i}.{h}")

            def conv_block(i):
                wait_drained(dve, f"proj{8 + i}")
                x = acc[:, 0:TP]
                tell(v.tensor_scalar(x, raw[:, 0:TP], wconv[:, 0, i:i + 1], None, ALU.mult))
                for t in range(1, 4):
                    tell(v.scalar_tensor_tensor(x, raw[:, t:t + TP], wconv[:, t, i:i + 1], x, ALU.mult, ALU.add),
                         "conv_ready" if t == 3 else None)
                if i % 6 == 5:
                    b = slice(i - 5, i + 1)
                    hh = hist[:, b, :].rearrange("p m (b t) -> p m b t", t=HIST)

                    def w(t):
                        return wconv[:, t, b].unsqueeze(2).broadcast_to([P, 6, TS])

                    tell(v.tensor_tensor(sacc[:], hh[:, :, :, 0], w(0), ALU.mult))
                    for t in range(1, 4):
                        src = hh[:, :, :, t] if t < 3 else tail[:, b, HIST:11]
                        tell(v.tensor_tensor(stmp[:], src, w(t), ALU.mult))
                        tell(v.tensor_tensor(sacc[:], sacc[:], stmp[:], ALU.add), "sample_acc" if t == 3 else None)

            def conf_taps(first_tap, n):
                for t in range(first_tap, min(first_tap + n, CK * CB)):
                    i, tap = divmod(t, CK)
                    x, w = cv[:, i, 0:TP], wdw[:, tap, i:i + 1]
                    if tap == 0:
                        tell(v.tensor_scalar(x, up[:, i, 0:TP], w, par[:, 32 + i:33 + i], ALU.mult, ALU.add))
                        p = vals[0][:, 0:TS * CK].rearrange("p (b t) -> p b t", b=TS)
                        tell(v.tensor_tensor(p, us[:, i, :, :], wdw[:, :, i].unsqueeze(1).broadcast_to([P, TS, CK]), ALU.mult))
                        tell(v.tensor_reduce(cv[:, i, TP:T], p, AX.X, ALU.add))
                        tell(v.tensor_scalar(cv[:, i, TP:T], cv[:, i, TP:T], par[:, 32 + i:33 + i], None, ALU.add))
                    else:
                        tell(v.scalar_tensor_tensor(x, up[:, i, tap:tap + TP], w, x, ALU.mult, ALU.add),
                             "conf_done" if t == CK * CB - 1 else None)

            def over_blocks(x):
                return x.unsqueeze(1).broadcast_to([P, CB, T])

            for kind, n, x in TIMETABLE:
                if kind == "block" and n:
                    what, i, _ = BLOCKS[n - 1]
                    name = f"proj{n - 1}"
                    if x == 0 and what == "sig":
                        wait_drained(dve, name)
                        wait_drained(dve, f"proj{n - 3}")
                        if i == 0:
                            dve.wait_ge(s["consts"], CONSTS)
                        tell(v.tensor_tensor(up[:, i, 30:286], vals[i % 2][:, 0:TP], sig[:, 0:TP], ALU.mult), "u_ready")
                        tell(v.tensor_tensor(us[:, i, :, CK - 1], vals[i % 2][:, TP:T], sig[:, TP:T], ALU.mult), "u_ready")
                    elif x == 0 and what == "qkv":
                        if i == 0:
                            wait_drained(dve, "par1")
                            wait_drained(dve, "par2")
                        conv_block(i)
                    elif x == 0 and what == "z":
                        dve.wait_ge(s["z_sig"], i + 1)
                        out_of(v.tensor_tensor(zT[:, i, :], bank[uses[name][0]][:, 0:T], sig, ALU.mult), name)
                    elif x == 2 and what == "qkv":
                        dve.wait_ge(s["silu_sig"], i + 1)
                        tell(v.tensor_tensor(qkvT[:, i, 0:TP], acc[:, 0:TP], sig[:, 0:TP], ALU.mult), "qkv_ready")
                        if i % 6 == 5:
                            dve.wait_ge(s["sample_sig"], i // 6 + 1)
                            tell(v.tensor_tensor(qkvT[:, i - 5:i + 1, TP:T], sacc[:], stmp[:], ALU.mult), "sample_ready")
                elif kind == "gdn":
                    gdn_step(n, x)
                elif kind == "conf_tap" and (n, x) in CONF_SLOTS:
                    conf_taps(CONF_SLOTS.index((n, x)) * TAPS_A_SLOT, TAPS_A_SLOT)
                elif kind == "conf_mean":
                    b = to_drain(dve, "cmu")
                    out_of(v.tensor_scalar(vals[0], b[:, 0:T], 1.0 / CC, None, ALU.mult), "cmu")
                    tell(v.tensor_tensor(cv[:], cv[:], over_blocks(vals[0]), ALU.subtract))
                    tell(v.tensor_tensor(conf_sq, cv[:], cv[:], ALU.mult), "csq")
                elif kind == "conf_var":
                    wait_drained(dve, "cvar")
                    tell(v.reciprocal(vals[1], vals[1]))
                    tell(v.tensor_tensor(cv[:], cv[:], over_blocks(vals[1]), ALU.mult))
                    for i in range(CB):
                        tell(v.tensor_scalar(cv[:, i, :], cv[:, i, :], par[:, 36 + i:37 + i], par[:, 40 + i:41 + i],
                                             ALU.mult, ALU.add), "caff" if i == CB - 1 else None)
                    dve.wait_ge(s["csig"], 1)
                    tell(v.tensor_tensor(cv[:], cv[:], conf_sq, ALU.mult), "cv_ready")

            tell(v.tensor_tensor(oT[:], oT[:], zT, ALU.mult), "onorm_ready")
            wait_drained(dve, f"proj{N_BLOCKS - 1}")
            wait_drained(dve, f"proj{N_BLOCKS - 2}")
            for i in range(KD):
                b = to_drain(dve, f"bb{i}")
                out_of(v.tensor_tensor(gbT[:, i, :], gbT[:, i, :], b[:, 0:T], ALU.mult), f"bb{i}")
            for i in range(KD):
                b = to_drain(dve, f"ba{i}")
                out_of(v.tensor_tensor(gaT[:, i, :], gaT[:, i, :], b[:, 0:T], ALU.mult), f"ba{i}")
                tell(v.tensor_tensor(aT[:, i, :], gaT[:, i, :], gbT[:, i, :], ALU.add), "mix")
            for i in range(KD):
                b = to_drain(dve, f"wo{i}")
                out_of(v.tensor_tensor(xT[:, i, :], xT[:, i, :], b[:, 0:T], ALU.add), f"wo{i}")
            norm("rms2", 8)

            for j in range(2):
                dve.wait_ge(s[f"state_stored{j}"], 16 * 4)
            b = to_drain(dve, "logits")
            for j in range(NTB):
                x = v.tensor_tensor(lg[:, j, 0:NE], b[0:TB, j * NE:(j + 1) * NE], brt[:], ALU.add)
                if j == NTB - 1:
                    out_of(x, "logits")
                else:
                    tell(x)
            tell(v.memset(lg[:, :, NE:NE + TOPK], BIG))
            for j in range(NTB):
                tell(v.max(m8[:, j, :], lg[:, j, 0:NE]))
            tell(v.tensor_scalar(nmax[:], m8[:, :, 0], -1.0, None, ALU.mult), "nmax")
            tell(v.memset(m8[:, :, TOPK:8], BIG))
            for j in range(NTB):
                tell(v.match_replace(rep[:, j, :], m8[:, j, :], lg[:, j, :], -BIG))
            tell(v.tensor_tensor(sel[:], rep[:, :, 0:NE], lg[:, :, 0:NE], ALU.not_equal), "selected")
            dve.wait_ge(s["wexp"], NTB)
            tell(v.tensor_tensor(gates[:], gates[:], sel[:], ALU.mult))
            tell(v.tensor_reduce(wsum[:], gates[:], AX.X, ALU.add))
            tell(v.reciprocal(wsum[:], wsum[:]))
            tell(v.tensor_tensor(gates[:], gates[:], wsum[:].unsqueeze(2).broadcast_to([TB, NTB, NE]), ALU.mult), "gates")
            b = to_drain(dve, "rank")
            r0 = rank[:, :, 0:NE]
            far = 10000.0
            tell(v.scalar_tensor_tensor(r0, b[0:TB, 0:NTB * NE].rearrange("p (j e) -> p j e", j=NTB), far, sel[:],
                                        ALU.add, ALU.mult))
            out_of(v.tensor_copy(cnt[:], b[:, NTB * NE:(NTB + 1) * NE]), "rank")
            tell(v.tensor_scalar(r0, r0, far, None, ALU.subtract))
            for j in range(1, PASSES):
                tell(v.tensor_scalar(rank[:, :, j * NE:(j + 1) * NE], r0, float(CAP * j), None, ALU.subtract))
            tell(v.tensor_reduce(cmax, cnt[:], AX.X, ALU.max))
            tell(v.tensor_copy(flag[:], cmax[0:1, :]), "flag_ready")
            for i in range(KD):
                b = to_drain(dve, f"bd{i}")
                out_of(v.tensor_tensor(xT[:, i, :], xT[:, i, :], b[:, 0:T], ALU.add), f"bd{i}")

            half = 4 * CAP
            PER = 6

            def four_of(x, h):
                return x[:, 4 * h:4 * h + 4, :]

            def make_onehot(sm, n, r):
                x = v.tensor_tensor(onehot[:], iota.unsqueeze(1).broadcast_to([TB, NTB, CAP]),
                                    rank[:, :, bass.ds(r, 1)].broadcast_to([TB, NTB, CAP]), ALU.is_equal)
                x.then_inc(sm["onehot"], 1)
                dve.wait_ge(sm["onehot"], n + 1)

            def expert(sm, n, e, r, first, last_one):
                own = [0]

                def then(x):
                    own[0] += 1
                    x.then_inc(sm["dve_e"], 1)
                    dve.wait_ge(sm["dve_e"], n * PER + own[0])

                if not first:
                    dve.wait_ge(sm["pt_filled"], n)
                x = v.tensor_tensor(gated[:], onehot[:], gates[:, :, bass.ds(e, 1)].broadcast_to([TB, NTB, CAP]), ALU.mult)
                x.then_inc(sm["gated"], 1)
                dve.wait_ge(sm["gated"], n + 1)
                if not last_one:
                    dve.wait_ge(sm["gather_filled"], n * 2 + 2)
                    make_onehot(sm, n + 1, r + 1)
                dve.wait_ge(sm["chunk_used"], n * RING_E + KD)
                for h in range(2):
                    x = bguT[:, 4 * h:4 * h + 4, bass.ds(e, 1)].broadcast_to([P, 4, CAP])
                    then(v.tensor_tensor(four_of(gbuf, h), bank[h][:, 0:half].rearrange("p (k c) -> p k c", k=4), x, ALU.add))
                v.tensor_scalar(gbuf[:], gbuf[:], LIMIT, None, ALU.min).then_inc(sm["gate_in"], 1)
                dve.wait_ge(sm["gate_in"], n + 1)
                for h in range(2):
                    x = bguT[:, 8 + 4 * h:12 + 4 * h, bass.ds(e, 1)].broadcast_to([P, 4, CAP])
                    then(v.tensor_tensor(four_of(ubuf, h), bank[2 + h][:, 0:half].rearrange("p (k c) -> p k c", k=4), x, ALU.add))
                then(v.tensor_scalar(ubuf[:], ubuf[:], LIMIT, -LIMIT, ALU.min, ALU.max))
                dve.wait_ge(sm["gate_sig"], n + 1)
                then(v.tensor_tensor(sbuf_sig[:], sbuf_sig[:], gbuf[:], ALU.mult))
                assert own[0] == PER
                v.scalar_tensor_tensor(gbuf[:], ubuf[:], 1.0, sbuf_sig[:], ALU.add, ALU.mult).then_inc(sm["hid"], 1)
                if not first:
                    add_back(sm, n - 1)

            def add_back(sm, n):
                for i in range(KD):
                    dve.wait_ge(sm["sc_filled"], n * 8 + i + 1)
                    v.tensor_tensor(xT[:, i, :], xT[:, i, :], bank[6 + i % 2][:, 0:T], ALU.add).then_inc(sm["sc_added"], 1)

            def run_experts(sm, base, r0):
                make_onehot(sm, base, r0)
                expert(sm, base, 0, r0, True, False)
                with dve.Fori(1, NE - 1) as e:
                    expert(sm, base + e, e, r0 + e, False, False)
                expert(sm, base + NE - 1, NE - 1, r0 + NE - 1, False, True)
                add_back(sm, base + NE - 1)

            dve.wait_ge(s["consts"], CONSTS + 2)
            run_experts(first, 0, 0)
            most = dve.value_load(flag[0:1, 0:1], min_val=0, max_val=T)
            with dve.If(most > CAP):
                dve.wait_ge(first["sc_added"], NE * KD)
                with dve.Fori(1, PASSES) as j:
                    run_experts(more, (j - 1) * NE, j * NE)
                dve.wait_ge(more["sc_added"], (PASSES - 1) * NE * KD)
            dve.wait_ge(first["sc_added"], NE * KD)

            norm("rms3", 16)
            for i in range(KD):
                wait_drained(dve, f"pg{i}")
                b = to_drain(dve, f"pp{i}")
                x = pieces[:, i % 2, :]
                out_of(v.tensor_tensor(x, x, b[:, 0:T], ALU.mult), f"pp{i}")
                tell(v.tensor_tensor(xT[:, i, :], xT[:, i, :], x, ALU.add), "x3")
            norm("rms4", 24)

        @block.gpsimd
        def _(pool):
            g_ = nc.gpsimd
            tell = Teller(pool, s, "pool_order")
            tell(g_.memset(ident[:], 0.0))
            tell(g_.affine_select(out=ident[:], in_=ident[:], compare_op=ALU.not_equal, fill=1.0, base=0,
                                  pattern=[[-1, P]], channel_multiplier=1))
            tell(g_.memset(ones[:], 1.0))
            tell(g_.affine_select(out=causal[:], in_=ones[:], compare_op=ALU.is_ge, fill=0.0, base=0,
                                  pattern=[[1, P]], channel_multiplier=-1), "consts")
            tell(g_.tensor_copy(sel8[:], ident[0:H, 0:H].unsqueeze(2).broadcast_to([H, H, P])), "consts")
            tell(g_.memset(raw[:, 0:HIST], 0.0))
            tell(g_.memset(eps[:, 0:1], NORM_EPS))
            tell(g_.memset(eps[:, 1:2], LN_EPS))
            tell(g_.memset(up[:, :, 0:CK - 1], 0.0), "consts")

            tell(g_.memset(neg_first[:], 0.0))
            x = neg_first[:].rearrange("p (a b) -> p a b", b=2)[:, :, 1]
            tell(g_.affine_select(out=x, in_=x, compare_op=ALU.not_equal, fill=-1.0, base=0,
                                  pattern=[[-2, P // 2]], channel_multiplier=1))
            tell(g_.memset(neg_mask[:], 0.0))
            for lv, side in enumerate(LEVELS + [P // 2]):
                n = P // (2 * side)
                x = neg_mask[:, lv, :].rearrange("p (a b i) -> p a b i", a=n, b=2)[:, :, 0, :]
                tell(g_.memset(x, -1.0))
                tell(g_.affine_select(out=x, in_=x, compare_op=ALU.is_ge, fill=0.0, base=-side,
                                      pattern=[[-2 * side, n], [0, side]], channel_multiplier=1))
                tell(g_.affine_select(out=x, in_=x, compare_op=ALU.is_ge, fill=0.0, base=2 * side - 1,
                                      pattern=[[2 * side, n], [0, side]], channel_multiplier=-1),
                     "masks_ready" if lv == len(LEVELS) else None)

            def gdn_step(g, step):
                qk4 = qkvT[:, 6 * g:6 * g + 4, :]
                if step == "norm":
                    pool.wait_ge(s["qkv_ready"], 6 * (g + 1))
                    pool.wait_ge(s["sample_ready"], g + 1)
                    if g:
                        wait_drained(pool, f"o.{g - 1}")
                        wait_drained(pool, f"s2.{g - 1}")
                        for j in range(2):
                            to_drain(pool, f"on{j}.{g - 1}")
                    tell(g_.tensor_tensor(nsq[:], qk4, qk4, ALU.mult), "nsq")
                elif step == "bcast":
                    pool.wait_ge(s["kb_ready"], 2 * (g + 1))
                    for j in range(2):
                        wait_drained(pool, f"bcg{j}.{g}")
                    tell(g_.tensor_tensor(kbg[:], kb[:], eg[:], ALU.mult), "kbg_ready")
                    tell(g_.tensor_tensor(qg[:], qkvT[:, 6 * g:6 * g + 2, :], eg[:], ALU.mult), "kbg_ready")
                elif step == "onorm":
                    wait_drained(pool, f"o.{g}")
                    pool.wait_ge(s["os_ready"], 2 * (g + 1))
                    o2 = oT[:, 2 * g:2 * g + 2, :]
                    tell(g_.tensor_tensor(osq[:], o2, o2, ALU.mult), "osq_ready")
                if SAMPLE_STEPS.get(step, ("", 0))[0] == "skq":
                    j = SAMPLE_STEPS[step][1]
                    to_drain(pool, f"skq.{2 * g + j}")
                    x = st[:, j, :, :]
                    tell(g_.tensor_tensor(x, x, eg[:, j, TP:T].unsqueeze(2).broadcast_to([P, TS, P]), ALU.mult), "sscaled")

            for kind, n, x in TIMETABLE:
                if kind == "gdn":
                    gdn_step(n, x)
            for j in range(2):
                pool.wait_ge(s[f"state_stored{j}"], 16 * 4)
            tell(g_.iota(iota_int, pattern=[[1, CAP]], base=0, channel_multiplier=0))
            tell(g_.tensor_copy(iota, iota_int), "consts")
            tell(g_.affine_select(out=before, in_=ones[0:TB, 0:TB], compare_op=ALU.is_ge, fill=0.0, base=-1,
                                  pattern=[[1, TB]], channel_multiplier=-1), "consts")


_INS = ["x_prompt", "x_sample", "p_prompt", "p_sample", "state_gdn", "state_qkv_conv", "state_conf_conv",
        "norm_mix", "w_in", "conv_qkv_w", "a_log", "dt_bias", "gdn_norm", "w_gdn_out", "conf_dw_w", "conf_dw_b",
        "conf_ln_g", "conf_ln_b", "w_conf_out", "w_out", "norm_ffn", "w_router", "b_router", "w_gate_up", "b_gate_up",
        "w_down", "b_down", "norm_ple", "w_ple_gate", "w_ple_proj", "norm_final"]
_OUTS = [(1, TP, D), (TS, 1, D), (1, 1, H, P, P), (1, 1, HIST, QKV), (1, 1, CK - 1, CC),
         (1, TS, H, P, P), (1, TS, HIST, QKV), (1, TS, CK - 1, CC)]


def kernel(**inputs):
    import numpy as np
    import concourse.bacc as bacc
    from concourse.bass_utils import run_bass_kernel_spmd as run

    nc = bacc.Bacc("TRN2", target_bir_lowering=False, num_devices=1)
    arrays, aps, outs = {}, {}, []
    for name in _INS:
        x = np.ascontiguousarray(inputs[name])
        arrays["in_" + name] = x
        aps[name] = nc.dram_tensor("in_" + name, x.shape, FP32, kind="ExternalInput").ap()
    for i, shape in enumerate(_OUTS):
        outs.append(nc.dram_tensor(f"out_{i}", shape, FP32, kind="ExternalOutput").ap())
    build(nc, aps, outs)
    r = run(nc, [arrays], core_ids=[0])
    return tuple(r.results[0][f"out_{i}"] for i in range(len(_OUTS)))
```

```python
import concourse.bass as bass
from concourse import mybir
from contextlib import ExitStack

FP32 = mybir.dt.float32
FP32R = mybir.dt.float32r
INT32 = mybir.dt.int32
ALU = mybir.AluOpType
ACT = mybir.ActivationFunctionType
AX = mybir.AxisListType

P = 128
D = 1024
KD = D // P
TP, TS = 256, 8
T = TP + TS
H = 8
HIST = 3
CC = 512
CB = CC // P
CK = 31
QKV = 3 * D
OFF_Z, OFF_BETA, OFF_A, OFF_GLU, OFF_GATE = 3072, 4096, 4104, 4112, 5136
NE, TOPK = 32, 4
PLE = 256
NORM_EPS, LN_EPS = 1e-6, 1e-5
LIMIT, ALPHA = 7.0, 1.702
PARAM_DMAS, ROW_DMAS = 13, 6
CONSTS = 3
CAP = 128
PASSES = -(-T // CAP)
TB = 88
NTB = T // TB
CHUNK = 128
LEVELS = [2, 4, 8, 16, 32]
BIG = 3.0e38

CHUNK_COLS = 2048
RING = 6
RING_A = 3
EXPERTS_EARLY = 30
CHUNKS = 12
PAIRS = 3
SCATTER_BANKS = [4, 5, 6, 7, 2, 3, 6, 7]
GPS_COLS = 512
DVE_LOWS, GPS_LOWS = 9, 11

GLU_ORDER = [("val", 0), ("val", 1), ("sig", 0), ("sig", 1), ("val", 2), ("val", 3), ("sig", 2), ("sig", 3)]
QKV_ORDER = [(kind, 2 * g + j) for g in range(4) for kind in range(3) for j in range(2)]


def _column_blocks():
    out = [(k, i, OFF_GLU + (CC if k == "sig" else 0) + P * i) for k, i in GLU_ORDER]
    out += [("qkv", n, kind * D + h * P) for n, (kind, h) in enumerate(QKV_ORDER)]
    out += [("z", h, OFF_Z + P * h) for h in range(H)]
    out += [("ga", i, OFF_GATE + P * i) for i in range(KD)]
    out += [("gb", i, OFF_GATE + D + P * i) for i in range(KD)]
    return out


BLOCKS = _column_blocks()
N_BLOCKS = len(BLOCKS)
GDN_STARTS = [3 * (15 + 6 * g) + 0 for g in range(4)]

GDN_STEPS = ["norm", "bcast", "scores", "tokens"]
for _lv in range(len(LEVELS)):
    GDN_STEPS += [f"ad{_lv}", f"dm{_lv}", f"tr{_lv}"]
GDN_STEPS += ["adl", "lt", "vn0", "s1", "ks", "vn1", "s2", "o", "onorm"]
GDN_JOBS = {"norm": ["n0", "n1", "n2", "n3"], "bcast": ["bcg0", "bcb0", "bcg1", "bcb1"],
            "scores": ["AT", "QK"], "tokens": ["kt", "vt", "T1"], "onorm": ["on0", "on1"]}
SAMPLE_STEPS = {"ad0": ("skq", 0), "ad1": ("srow", 0), "ad2": ("kv", 0),
                "ad3": ("skq", 1), "ad4": ("srow", 1), "adl": ("kv", 1)}


def _timetable():
    out = []
    for n in range(N_BLOCKS + 1):
        for third in range(3):
            out.append(("block", n, third))
            for g, start in enumerate(GDN_STARTS):
                if 0 <= 3 * n + third - start < len(GDN_STEPS):
                    out.append(("gdn", g, GDN_STEPS[3 * n + third - start]))
            if third == 1:
                if n in (12, 13):
                    out.append(("conf_rows", n - 12, 0))
                if 34 <= n < 40:
                    out.append(("tail", n - 34, 0))
                if n == 50:
                    out.append(("conf_mean", 0, 0))
                if n == 52:
                    out.append(("conf_var", 0, 0))
            if n >= 12:
                out.append(("conf_tap", n, third))
    return out


TIMETABLE = _timetable()
CONF_SLOTS = [(i[1], i[2]) for i in TIMETABLE if i[0] == "conf_tap" and i[1] < 48 for _ in range(1 if i[1] < 40 else 2)]
assert len(CONF_SLOTS) >= CK * CB

SEMAPHORES = """consts x_loaded params_loaded ba_loaded late_loaded bd_loaded rows_loaded squares rstd_ready aT_ready
 act_order dve_order pool_order conv_ready silu_sig qkv_ready sample_acc sample_sig u_ready z_sig
 gates_in b_high bias_ready e1_ready sp_in ln_ready expa gT_ready esc_in esc_ready gcF_ready nsq nrstd nrm dec_diff
 dec_exp kb_ready kbg_ready DT0_ready osq_ready orstd_ready onorm_ready kq_ready sample_ready
 state_loaded0 state_loaded1 svn_ready os_ready sscaled state_stored0 state_stored1 sfin_stored
 masks_ready conf_done csq crstd caff csig cv_ready mix tail_stored nmax wexp gates
 selected rank inverse_norms inverse_ostd flag_ready outs x3""".split()

EXPERT_SEMAPHORES = """onehot gated selector gather_filled x_high x_low high low_dve low_gps gate_in gate_sig
 hid ht_filled h_high h_low y_high y_low sc_filled sc_added pt_filled slot_gate spread chunk_used dve_e""".split()


class Teller:

    def __init__(self, engine, sems, own):
        self.engine, self.sems, self.own = engine, sems, own
        self.count = {}

    def __call__(self, instruction, name=None):
        name = name or self.own
        self.count[name] = self.count.get(name, 0) + 1
        instruction.then_inc(self.sems[name], 1)
        self.engine.wait_ge(self.sems[name], self.count[name])


def build(nc, a, out):
    with ExitStack() as ctx:
        def sbuf(name, shape, dt=FP32):
            return ctx.enter_context(nc.sbuf_tensor(name, shape, dt))

        s = {n: ctx.enter_context(nc.semaphore(n)) for n in SEMAPHORES}
        first = {n: ctx.enter_context(nc.semaphore("e_" + n)) for n in EXPERT_SEMAPHORES}
        more = {n: ctx.enter_context(nc.semaphore("m_" + n)) for n in EXPERT_SEMAPHORES}
        loaded = [ctx.enter_context(nc.semaphore(f"slot_loaded_{i}")) for i in range(RING)]
        more_loaded = [ctx.enter_context(nc.semaphore(f"slot_loaded_more_{i}")) for i in range(RING)]
        filled = [ctx.enter_context(nc.semaphore(f"bank_filled_{i}")) for i in range(8)]
        drained = [ctx.enter_context(nc.semaphore(f"bank_drained_{i}")) for i in range(8)]

        def with_split_view(name, cols, split_name, shape):
            t = sbuf(name, [P, cols])
            at = nc.sbuf_base - 4 * cols
            return t, nc.alloc_sbuf_tensor_at(split_name, shape, FP32R, offset=at, align_bytes=32)

        ring = sbuf("ring", [P, RING, CHUNK_COLS])
        upper, pairs = with_split_view("upper", PAIRS * 2 * CHUNK_COLS, "pairs", [P, PAIRS, 2, CHUNK_COLS])

        def carve(base, start, *shape):
            n = 1
            for x in shape:
                n *= x
            v = base[:, start:start + n]
            if len(shape) == 2:
                v = v.rearrange("p (a b) -> p a b", a=shape[0])
            elif len(shape) == 3:
                v = v.rearrange("p (a b c) -> p a b c", a=shape[0], b=shape[1])
            return v

        qkvT = carve(upper, 0, 24, T)
        at = 24 * T
        lent_slots = ring[:, RING_A:RING, :].rearrange("p s c -> p (s c)")

        def work_space(base, at):
            four = [carve(base, at + 512 * i, 4, P) for i in range(8)]
            kb, kbg, qg = (carve(base, at + 4096 + 528 * i, 2, T) for i in range(3))
            S1 = carve(base, at + 4096 + 1584, 2, P)
            nsq = carve(base, at + 4096, 4, T)
            nstd = carve(base, at, 4, T)
            return four + [kb, kbg, qg, S1, nsq, nstd]

        work = [work_space(upper, at), work_space(lent_slots, 0)]

        xs = carve(upper, at, 3, D)
        ps_tok = carve(upper, at + 3072, 3, PLE)
        stage = carve(upper, at + 3072 + 768, 3, P)

        big = sbuf("big", [P, 3 * KD * T])
        zT = carve(big, 0, H, T)
        gaT = carve(big, KD * T, KD, T)
        gbT = carve(big, 2 * KD * T, KD, T)
        hist_rows = big[0:TS * HIST, 0:QKV]
        conf_rows = carve(big, QKV, 2, CC)
        hm_tok = carve(big, 0, NTB, D)
        gbuf, ubuf, gsig = (carve(big, (NTB + i) * D, D) for i in range(3))
        b_down = gbuf[0:NE, :]
        b_stage = carve(big, (NTB + 1) * D, 2 * D)[0:2 * NE, :]

        xT = sbuf("xT", [P, KD, T])
        outputs, moe_y = with_split_view("outputs", (H + 5) * T, "moe_y", [P, 2 * D + T])
        oT = carve(outputs, 0, H, T)
        CONF = CB * 286 + CB * 248
        lent, moe = with_split_view("lent", CONF + CB * T + 24 * (TS * HIST + 11) + KD * T, "moe",
                                    [P, 2 * D + 4 * KD * CAP])
        conf = carve(lent, 0, CONF)
        cv = carve(lent, CONF, CB, T)
        hist = carve(lent, CONF + CB * T, 24, TS * HIST)
        tail = carve(lent, CONF + CB * T + 24 * TS * HIST, 24, 11)
        aT = carve(lent, CONF + CB * T + 24 * (TS * HIST + 11), KD, T)
        bias = moe[0:2 * NE, 0:2 * D]
        x_high, x_low, h_high, h_low = (moe[:, 2 * D + i * KD * CAP:2 * D + (i + 1) * KD * CAP]
                                        .rearrange("p (k c) -> p k c", k=KD) for i in range(4))
        up = carve(conf, 0, CB, 286)
        us = carve(conf, CB * 286, CB, TS, CK)
        conf_sq = carve(conf, 0, CB, T)
        pieces = carve(outputs, H * T, 5, T)
        raw = pieces[:, 0, :]
        acc = pieces[:, 1, :]
        sig = pieces[:, 2, :]
        vals = [pieces[:, 3, :], pieces[:, 4, :]]
        sacc = sbuf("sacc", [P, 6, TS])
        stmp = sbuf("stmp", [P, 6, TS])
        par = sbuf("par", [P, 45])
        wconv = sbuf("wconv", [P, 4, 24])
        wdw = sbuf("wdw", [P, CK, CB])
        ident = sbuf("ident", [P, P])
        ones = sbuf("ones", [P, P])
        causal = sbuf("causal", [P, P])
        neg_first = sbuf("neg_first", [P, P])
        neg_mask = sbuf("neg_mask", [P, len(LEVELS) + 1, P])
        sel8 = sbuf("sel8", [H, H, P])
        eye2 = sbuf("eye2", [2 * NE, NE])
        selector = sbuf("selector", [2 * NE, CAP], FP32R)
        rows8 = sbuf("rows8", [H, 2, T])
        betaT, gcF = rows8[:, 0, :], rows8[:, 1, :]
        gT, tmp8, tmp8b = acc[0:H], vals[0][0:H], vals[1][0:H]
        small8 = sbuf("small8", [H, 4])
        gbt = sbuf("gbt", [P, 4, H])
        gct = sbuf("gct", [P, 4, H])
        esc = sbuf("esc", [P, 4, H])
        eg = sbuf("eg", [P, 2, T])
        beta_s = sbuf("beta_s", [P, 2, TS])
        kq = sbuf("kq", [P, 2, TS, 2])
        qk_s = sbuf("qk_s", [P, 2, TS])
        sv = sbuf("sv", [P, 4, TS])
        rstd = sbuf("rstd", [P, T])
        ostd = sbuf("ostd", [P, 2, T])
        st = sbuf("st", [P, 2, TS, P])
        krow = sbuf("krow", [TS, P])
        vbd = sbuf("vbd", [TS, TS, P])
        sfin = sbuf("sfin", [P, 2, P])
        qrow = sbuf("qrow", [CK - 1, 4 * P])
        pT = sbuf("pT", [P, 2, T])
        wr = sbuf("wr", [P, KD, NE])
        wba = sbuf("wba", [P, KD, 2 * H])
        brt = sbuf("brt", [TB, NE])
        eps = sbuf("eps", [P, 2])
        flag = sbuf("flag", [1, 1], INT32)
        slots = st[:].rearrange("p a b c -> p (a b c)")
        at = [0]

        def small(*shape):
            v = carve(slots, at[0], *shape)
            n = 1
            for x in shape:
                n *= x
            at[0] += n + n % 2
            return v

        lg, rep = small(NTB, NE + TOPK)[0:TB], small(NTB, NE + TOPK)[0:TB]
        m8 = small(NTB, 8)[0:TB]
        nmax, wsum = small(NTB)[0:TB], small(NTB)[0:TB]
        sel, gates = small(NTB, NE)[0:TB], small(NTB, NE)[0:TB]
        rank = small(NTB, PASSES * NE)[0:TB]
        onehot, gated = small(NTB, CAP)[0:TB], small(NTB, CAP)[0:TB]
        iota, iota_int = small(CAP)[0:TB], gated[:, 0, :].bitcast(INT32)
        cnt, cmax = small(NE), small(1)
        gatesT = small(T)[0:NE]
        before = small(TB)[0:TB]
        assert at[0] <= 2 * TS * P
        y_high, y_low = moe_y[0:CAP, 0:D], moe_y[0:CAP, D:2 * D]
        spread = moe_y[0:CAP, 2 * D:2 * D + T]
        slot_gate = sbuf("slot_gate", [CAP, 1])
        yrows = big[:, 0:3 * D].rearrange("p (t d) -> p t d", t=3)

        bank = [ctx.enter_context(nc.psum_tensor(f"bank{i}", [P, 512], FP32)) for i in range(8)]

        uses = {}
        count = [0] * 8
        turn = [0]

        def plan(name, b):
            uses[name] = (b, count[b])
            count[b] += 1

        early = ["par0", "par1", "par2"] + [f"x{t}{h}" for t in range(3) for h in range(2)]
        early += ["rms1", "hist0", "hist1", "ch0", "ch1", "pT", "pTs", "beta", "a", "gbt", "gct", "gcf"]
        for i, n in enumerate(early):
            plan(n, 2 + i % 6)
        for kind, n, x in TIMETABLE:
            if kind == "block" and x == 0 and n < N_BLOCKS:
                plan(f"proj{n}", n % 2)
            elif kind == "gdn":
                for job in GDN_JOBS.get(x, [x]):
                    plan(f"{job}.{n}", 2 + turn[0] % 4)
                    turn[0] += 1
                if x in SAMPLE_STEPS:
                    step, j = SAMPLE_STEPS[x]
                    if step == "kv":
                        plan(f"kv0.{2 * n + j}", 6)
                        plan(f"kv1.{2 * n + j}", 7)
                    else:
                        plan(f"{step}.{2 * n + j}", 6 if step == "skq" else 7)
            elif kind == "conf_rows":
                plan(f"crow{n}", 6 + n)
            elif kind == "tail":
                plan(f"tail{n}", 6 + n % 2)
            elif kind == "conf_mean":
                plan("cmu", 6)
            elif kind == "conf_var":
                plan("cvar", 7)
        for name in ("bb", "ba", "wo"):
            for i in range(KD):
                plan(f"{name}{i}", i)
        plan("rms2", 0)
        plan("logits", 1)
        for i in range(6):
            plan(f"hm{i}", 2 + i)
        plan("gTr", 0)
        plan("rank", 1)
        for i in range(KD):
            plan(f"bd{i}", i)
        before_experts = list(count)
        plan("rms3", 0)
        for i in range(KD):
            plan(f"pg{i}", 4 * (i % 2) + 1)
            plan(f"pp{i}", 4 * (i % 2) + 2)
        plan("rms4", 0)
        for t in range(3):
            for h in range(2):
                plan(f"y{t}{h}", 2 + 2 * t + h)

        def to_fill(pe, name):
            b, k = uses[name]
            if k:
                pe.wait_ge(drained[b], k)
            return bank[b][:]

        def fill_done(name, instruction):
            instruction.then_inc(filled[uses[name][0]], 1)

        def to_drain(engine, name):
            b, k = uses[name]
            engine.wait_ge(filled[b], k + 1)
            return bank[b][:]

        def drain_sem(name):
            return drained[uses[name][0]]

        def wait_drained(engine, name):
            b, k = uses[name]
            engine.wait_ge(drained[b], k + 1)

        w_in = a["w_in"][0]

        def cols(w, c0, n=256):
            return w[:, c0:c0 + n].rearrange("(k p) c -> p k c", p=P)

        stream = [("in", BLOCKS[2 * i][2]) for i in range(N_BLOCKS // 2)]
        stream += [("conf", i) for i in range(2)] + [("gdn", i) for i in range(4)] + [("out", i) for i in range(4)]
        first_use = {}
        for n, (kind, i) in enumerate(stream):
            first_use[(kind, i)] = n
        slot_fills = [len(range(i, len(stream), RING_A)) for i in range(RING_A)] + [0] * (RING - RING_A)

        def chunk_view(kind, slot):
            v = ring[:, slot, :]
            k = {"in": KD, "gdn": KD, "out": KD, "conf": CB, "down": 2}[kind]
            return v.rearrange("p (k c) -> p k c", k=k)

        def take_chunk(pe, kind, i):
            n = first_use[(kind, i)]
            pe.wait_ge(loaded[n % RING_A], 16 * (n // RING_A + 1))
            return chunk_view(kind, n % RING_A)

        def wait_used(engine, n):
            kind, i = stream[n]
            if kind == "in":
                name = f"proj{2 * n + 1}"
            else:
                name = {"conf": f"bb{4 * i + 3}", "gdn": f"ba{2 * i + 1}", "out": f"wo{2 * i + 1}"}[kind]
            to_drain(engine, name)

        def slot_of(c):
            c = c % RING
            return RING_A + c if c < RING - RING_A else (len(stream) + c - (RING - RING_A)) % RING_A

        def raw_chunk(c):
            return ring[:, slot_of(c), :]

        def pair(c, low):
            return pairs[:, c % PAIRS, low, :]

        def wait_high(engine, sm, n, c):
            engine.wait_ge(sm["high"], n * CHUNKS + (c + 1))

        def wait_chunk_used(sp, sm, n, c):
            sp.wait_ge(sm["chunk_used"], n * CHUNKS + (c + 1))

        def wait_low(engine, sm, n, c):
            dve_lows, gps_lows = n * DVE_LOWS + min(c + 1, DVE_LOWS), n * GPS_LOWS + min(c + 1, GPS_LOWS)
            if c < KD or c == CHUNKS - 1:
                engine.wait_ge(sm["low_dve"], dve_lows)
            if c < CHUNKS - 1:
                engine.wait_ge(sm["low_gps"], gps_lows)

        block = ctx.enter_context(nc.Block())

        @block.sync
        def _(sp):
            sp.dma_start(wba[:], w_in[:, OFF_BETA:OFF_GLU].rearrange("(k p) c -> p k c", p=P)).then_inc(s["ba_loaded"], 16)
            sp.dma_start(wr[:], a["w_router"][0].rearrange("(k p) c -> p k c", p=P)).then_inc(s["ba_loaded"], 16)
            w_gu, w_dn = a["w_gate_up"][0], a["w_down"][0]

            def load_chunk(e, c, sems):
                if c < KD:
                    dst, src = raw_chunk(c), w_gu[e, c * P:(c + 1) * P, :]
                else:
                    r = 2 * P * (c - KD)
                    dst = raw_chunk(c).rearrange("p (k d) -> p k d", k=2)
                    src = w_dn[e, r:r + 2 * P, :].rearrange("(k p) d -> p k d", p=P)
                sp.dma_start(dst, src).then_inc(sems[slot_of(c)], 16)

            def load_expert(e, n, sems, sm, skip_wait):
                for c in range(CHUNKS):
                    if c >= RING:
                        wait_chunk_used(sp, sm, n, c - RING)
                    elif not skip_wait:
                        wait_chunk_used(sp, sm, n - 1, c + CHUNKS - RING)
                    load_chunk(e, c, sems)

            for n, (kind, i) in enumerate(stream):
                if n == EXPERTS_EARLY:
                    wait_drained(sp, "o.3")
                    wait_drained(sp, "s2.3")
                    sp.wait_ge(s["os_ready"], H)
                    sp.wait_ge(s["kbg_ready"], H)
                    sp.wait_ge(s["onorm_ready"], 4)
                    for c in range(RING - RING_A):
                        load_chunk(0, c, loaded)
                slot = n % RING_A
                if n >= RING_A:
                    wait_used(sp, n - RING_A)
                if kind == "in":
                    src = cols(w_in, i)
                elif kind == "conf":
                    src = cols(a["w_conf_out"][0], 512 * i, 512)
                elif kind == "gdn":
                    src = cols(a["w_gdn_out"][0], 256 * i)
                else:
                    src = cols(a["w_out"][0], 256 * i)
                sp.dma_start(chunk_view(kind, slot), src).then_inc(loaded[slot], 16)
            for c in range(RING - RING_A, RING):
                wait_used(sp, len(stream) - RING + c)
                load_chunk(0, c, loaded)
            for c in range(RING, CHUNKS):
                wait_chunk_used(sp, first, 0, c - RING)
                load_chunk(0, c, loaded)
            with sp.Fori(1, NE) as e:
                load_expert(e, e, loaded, first, False)
            sp.wait_ge(s["flag_ready"], 1)
            most = sp.value_load(flag[0:1, 0:1], min_val=0, max_val=T)
            with sp.If(most > CAP):
                for c in range(CHUNKS - RING, CHUNKS):
                    wait_chunk_used(sp, first, NE - 1, c)
                load_expert(0, 0, more_loaded, more, True)
                with sp.Fori(1, NE) as e:
                    load_expert(e, e, more_loaded, more, False)
                with sp.Fori(2, PASSES) as j:
                    with sp.Fori(0, NE) as e:
                        load_expert(e, (j - 1) * NE + e, more_loaded, more, False)
                for c in range(CHUNKS - RING, CHUNKS):
                    wait_chunk_used(sp, more, (PASSES - 1) * NE - 1, c)
            for c in range(5):
                wait_chunk_used(sp, first, NE - 1, c + CHUNKS - RING)
                if c < 4:
                    sp.dma_start(chunk_view("in", slot_of(c)), cols(a["w_ple_gate"][0], 256 * c)).then_inc(s["late_loaded"], 16)
                else:
                    sp.dma_start(chunk_view("down", slot_of(c)),
                                 a["w_ple_proj"][0].rearrange("(k p) d -> p k d", p=P)).then_inc(s["late_loaded"], 16)

        def q_of(g, j):
            return qkvT[:, 6 * g + j, :]

        def k_of(g, j):
            return qkvT[:, 6 * g + 2 + j, :]

        def v_of(g, j):
            return qkvT[:, 6 * g + 4 + j, :]

        def chunk(v, c):
            return v[:, c * CHUNK:(c + 1) * CHUNK]

        @block.tensor
        def _(pe):
            mm, tr = nc.tensor.matmul, nc.tensor.transpose

            pe.wait_ge(s["consts"], CONSTS)
            pe.wait_ge(s["params_loaded"], 16 * PARAM_DMAS)
            for i, rows in enumerate((45, 96, 124)):
                b = to_fill(pe, f"par{i}")
                fill_done(f"par{i}", tr(b[:, 0:rows], stage[0:rows, i, :], ident[0:rows, 0:rows]))
            pe.wait_ge(s["x_loaded"], 16 * 3)
            for t in range(3):
                w = P if t < 2 else TS
                for h in range(2):
                    b = to_fill(pe, f"x{t}{h}")
                    for i in range(4):
                        k = 4 * h + i
                        last = tr(b[:, i * w:(i + 1) * w], xs[0:w, t, k * P:(k + 1) * P], ident[0:w, 0:w])
                    fill_done(f"x{t}{h}", last)

            def sum_squares(name, n):
                x = aT if n == 1 else zT
                b = to_fill(pe, name)
                for k in range(KD):
                    pe.wait_ge(s["squares"], KD * (n - 1) + k + 1)
                    last = mm(b[:, 0:T], ones[:], x[:, k, :], start=k == 0, stop=k == KD - 1)
                fill_done(name, last)

            def wait_block(n, k):
                pe.wait_ge(s["aT_ready"], KD * (n - 1) + k + 1)

            sum_squares("rms1", 1)
            pe.wait_ge(s["rows_loaded"], 16 * ROW_DMAS)
            R = TS * HIST
            for i in range(2):
                b = to_fill(pe, f"hist{i}")
                for m in range(12):
                    kind, h = QKV_ORDER[12 * i + m]
                    c0 = kind * D + h * P
                    last = tr(b[:, m * R:(m + 1) * R], hist_rows[:, c0:c0 + P], ident[0:R, 0:R])
                fill_done(f"hist{i}", last)
            for i in range(2):
                b = to_fill(pe, f"ch{i}")
                for m in range(CB):
                    last = tr(b[:, m * 120:(m + 1) * 120], conf_rows[0:120, i, m * P:(m + 1) * P], ident[0:120, 0:120])
                fill_done(f"ch{i}", last)
            b = to_fill(pe, "pT")
            for t in range(2):
                for k in range(2):
                    last = tr(b[:, k * TP + t * P:k * TP + (t + 1) * P], ps_tok[:, t, k * P:(k + 1) * P], ident[:])
            fill_done("pT", last)
            b = to_fill(pe, "pTs")
            for k in range(2):
                last = tr(b[:, k * TS:(k + 1) * TS], ps_tok[0:TS, 2, k * P:(k + 1) * P], ident[0:TS, 0:TS])
            fill_done("pTs", last)

            pe.wait_ge(s["ba_loaded"], 16 * 2)
            wait_block(1, KD - 1)
            for name, o in (("beta", 0), ("a", H)):
                b = to_fill(pe, name)
                for k in range(KD):
                    last = mm(b[0:H, 0:T], wba[:, k, o:o + H], aT[:, k, :], start=k == 0, stop=k == KD - 1)
                fill_done(name, last)
            pe.wait_ge(s["gT_ready"], 1)
            wait_drained(pe, "beta")
            b = to_fill(pe, "gbt")
            for i, src in enumerate((gT, gT, betaT, betaT)):
                last = tr(b[:, i * H:(i + 1) * H], chunk(src, i % 2), ident[0:H, 0:H])
            fill_done("gbt", last)
            wait_drained(pe, "gbt")
            b = to_fill(pe, "gct")
            for i in range(4):
                last = mm(b[:, i * H:(i + 1) * H], (causal if i < 2 else ones)[:], gbt[:, i % 2, :], start=True, stop=True)
            fill_done("gct", last)
            b = to_fill(pe, "gcf")
            for c in range(2):
                last = mm(b[0:H, c * CHUNK:(c + 1) * CHUNK], gbt[:, c, :], causal[:], start=True, stop=True)
            fill_done("gcf", last)

            def products4(name, lhs, rhs):
                b = to_fill(pe, name)
                for i in range(4):
                    last = mm(b[:, i * P:(i + 1) * P], lhs(i), rhs(i), start=True, stop=True)
                fill_done(name, last)

            def transposes4(name, src):
                b = to_fill(pe, name)
                for i in range(4):
                    last = tr(b[:, i * P:(i + 1) * P], src(i), ident[:])
                fill_done(name, last)

            def gdn_step(g, step):
                def name(x):
                    return f"{x}.{g}"

                AT, Dm, DT, M, QKT, kd, vb, dec, kb, kbg, qg, S1, nsq, nstd = work[g % 2]
                vn, osq = M, kb
                if step == "norm":
                    pe.wait_ge(s["nsq"], g + 1)
                    for i in range(4):
                        b = to_fill(pe, name(f"n{i}"))
                        fill_done(name(f"n{i}"), mm(b[:, 0:T], ones[:], nsq[:, i, :], start=True, stop=True))
                elif step == "bcast":
                    pe.wait_ge(s["gcF_ready"], 1)
                    wait_drained(pe, "gcf")
                    wait_drained(pe, "beta")
                    for j in range(2):
                        for x, src in (("bcg", gcF), ("bcb", betaT)):
                            b = to_fill(pe, name(f"{x}{j}"))
                            fill_done(name(f"{x}{j}"), mm(b[:, 0:T], sel8[:, 2 * g + j, :], src, start=True, stop=True))
                elif step == "scores":
                    pe.wait_ge(s["nrm"], 2 * (g + 1))
                    pe.wait_ge(s["kb_ready"], 2 * (g + 1))
                    products4(name("AT"), lambda i: chunk(k_of(g, i // 2), i % 2), lambda i: chunk(kb[:, i // 2, :], i % 2))
                    products4(name("QK"), lambda i: chunk(k_of(g, i // 2), i % 2), lambda i: chunk(q_of(g, i // 2), i % 2))
                elif step == "tokens":
                    transposes4(name("kt"), lambda i: chunk(k_of(g, i // 2), i % 2))
                    transposes4(name("vt"), lambda i: chunk(v_of(g, i // 2), i % 2))
                    pe.wait_ge(s["DT0_ready"], g + 1)
                    transposes4(name("T1"), lambda i: DT[:, i, :])
                elif step[:2] == "ad":
                    lv = len(LEVELS) if step == "adl" else int(step[2])
                    wait_drained(pe, name(f"dm{lv - 1}" if lv else "T1"))
                    wait_drained(pe, name("AT"))
                    products4(name(step), lambda i: AT[:, i, :], lambda i: Dm[:, i, :])
                elif step[:2] == "dm":
                    lv = int(step[2])
                    wait_drained(pe, name(f"ad{lv}"))
                    if lv:
                        wait_drained(pe, name(f"tr{lv - 1}"))
                    products4(name(step), lambda i: DT[:, i, :], lambda i: M[:, i, :])
                elif step[:2] == "tr":
                    wait_drained(pe, name(f"dm{step[2]}"))
                    transposes4(name(step), lambda i: Dm[:, i, :])
                elif step == "lt":
                    wait_drained(pe, name("adl"))
                    wait_drained(pe, name(f"tr{len(LEVELS) - 1}"))
                    products4(name("lt"), lambda i: M[:, i, :], lambda i: DT[:, i, :])
                elif step in ("vn0", "vn1"):
                    c = int(step[2])
                    wait_drained(pe, name("lt"))
                    wait_drained(pe, name("kt"))
                    wait_drained(pe, name("vt"))
                    if c:
                        wait_drained(pe, name("ks"))
                    b = to_fill(pe, name(step))
                    for j in range(2):
                        last = mm(b[:, j * P:(j + 1) * P], DT[:, 2 * j + c, :], vb[:, 2 * j + c, :], start=True, stop=True)
                    fill_done(name(step), last)
                elif step in ("s1", "s2"):
                    c = int(step[1]) - 1
                    wait_drained(pe, name(f"vn{c}"))
                    b = to_fill(pe, name(step))
                    for j in range(2):
                        last = mm(b[:, j * P:(j + 1) * P], kd[:, 2 * j + c, :], vn[:, 2 * j + c, :], start=True, stop=True)
                    fill_done(name(step), last)
                elif step == "ks":
                    wait_drained(pe, name("s1"))
                    pe.wait_ge(s["kbg_ready"], 2 * (g + 1))
                    b = to_fill(pe, name(step))
                    for j in range(2):
                        last = mm(b[:, j * P:(j + 1) * P], chunk(kbg[:, j, :], 1), S1[:, j, :], start=True, stop=True)
                    fill_done(name(step), last)
                elif step == "o":
                    wait_drained(pe, name("QK"))
                    b = to_fill(pe, name(step))
                    for j in range(2):
                        o = 2 * j * P
                        mm(b[:, o:o + P], vn[:, 2 * j, :], QKT[:, 2 * j, :], start=True, stop=True)
                        mm(b[:, o + P:o + 2 * P], S1[:, j, :], chunk(qg[:, j, :], 1), start=True, stop=False)
                        last = mm(b[:, o + P:o + 2 * P], vn[:, 2 * j + 1, :], QKT[:, 2 * j + 1, :], start=False, stop=True)
                    fill_done(name(step), last)
                elif step == "onorm":
                    pe.wait_ge(s["osq_ready"], g + 1)
                    for j in range(2):
                        b = to_fill(pe, name(f"on{j}"))
                        fill_done(name(f"on{j}"), mm(b[:, 0:T], ones[:], osq[:, j, :], start=True, stop=True))
                if step in SAMPLE_STEPS:
                    sample_step(g, *SAMPLE_STEPS[step])

            def sample_step(g, step, j):
                h = 2 * g + j
                if step == "skq":
                    pe.wait_ge(s[f"state_loaded{j}"], 16 * (g + 1))
                    pe.wait_ge(s["kq_ready"], g + 1)
                    b = to_fill(pe, f"skq.{h}")
                    for i in range(TS):
                        mm(b[:, 2 * i:2 * i + 2], st[:, j, i, :], kq[:, j, i, :], start=True, stop=True)
                    fill_done(f"skq.{h}", mm(b[:, 16:24], ones[:], qk_s[:, j, :], start=True, stop=True))
                elif step == "srow":
                    pe.wait_ge(s["svn_ready"], h + 1)
                    b = to_fill(pe, f"srow.{h}")
                    tr(b[0:TS, 0:P], k_of(g, j)[:, TP:T], ident[:])
                    fill_done(f"srow.{h}", tr(b[0:TS, P:2 * P], sv[:, 2, :], ident[:]))
                else:
                    wait_drained(pe, f"srow.{h}")
                    for i in range(2):
                        b = to_fill(pe, f"kv{i}.{h}")
                        fill_done(f"kv{i}.{h}", mm(b[:], krow[:], vbd[:, 4 * i:4 * i + 4, :].rearrange("b i v -> b (i v)"),
                                                   start=True, stop=True))

            for kind, n, x in TIMETABLE:
                if kind == "block" and n < N_BLOCKS:
                    if x == 0:
                        b = to_fill(pe, f"proj{n}")
                        if n % 2 == 0:
                            w = take_chunk(pe, "in", BLOCKS[n][2])
                        o = P * (n % 2)
                    for k in ((0, 1, 2), (3, 4, 5), (6, 7))[x]:
                        last = mm(b[:, 0:T], w[:, k, o:o + P], aT[:, k, :], start=k == 0, stop=k == KD - 1)
                    if x == 2:
                        fill_done(f"proj{n}", last)
                elif kind == "gdn":
                    keep = b
                    gdn_step(n, x)
                    b = keep
                elif kind == "conf_rows":
                    pe.wait_ge(s["u_ready"], 8)
                    bb = to_fill(pe, f"crow{n}")
                    for i in range(CB):
                        if n == 0:
                            last = tr(bb[0:30, i * P:(i + 1) * P], up[:, i, 256:286], ident[:])
                        else:
                            last = tr(bb[0:TS, i * P:(i + 1) * P], us[:, i, :, CK - 1], ident[:])
                    fill_done(f"crow{n}", last)
                elif kind == "tail":
                    wait_drained(pe, f"proj{8 + 22}")
                    wait_drained(pe, f"proj{8 + 23}")
                    bb = to_fill(pe, f"tail{n}")
                    for i in range(4):
                        m = QKV_ORDER.index(divmod(4 * n + i, H))
                        last = tr(bb[0:11, i * P:(i + 1) * P], tail[:, m, :], ident[:])
                    fill_done(f"tail{n}", last)
                elif kind == "conf_mean":
                    pe.wait_ge(s["conf_done"], 1)
                    bb = to_fill(pe, "cmu")
                    for i in range(CB):
                        last = mm(bb[:, 0:T], ones[:], cv[:, i, :], start=i == 0, stop=i == CB - 1)
                    fill_done("cmu", last)
                elif kind == "conf_var":
                    pe.wait_ge(s["csq"], 1)
                    bb = to_fill(pe, "cvar")
                    for i in range(CB):
                        last = mm(bb[:, 0:T], ones[:], conf_sq[:, i, :], start=i == 0, stop=i == CB - 1)
                    fill_done("cvar", last)

            def dense(name, kind, per, n_k, rhs):
                for i in range(KD):
                    w = take_chunk(pe, kind, i // per)
                    b = to_fill(pe, f"{name}{i}")
                    o = P * (i % per)
                    for k in range(n_k):
                        last = mm(b[:, 0:T], w[:, k, o:o + P], rhs(k), start=k == 0, stop=k == n_k - 1)
                    fill_done(f"{name}{i}", last)

            pe.wait_ge(s["cv_ready"], 1)
            dense("bb", "conf", 4, CB, lambda k: cv[:, k, :])
            pe.wait_ge(s["onorm_ready"], 5)
            dense("ba", "gdn", 2, H, lambda k: oT[:, k, :])
            pe.wait_ge(s["mix"], KD)
            dense("wo", "out", 2, KD, lambda k: aT[:, k, :])

            sum_squares("rms2", 2)
            b = to_fill(pe, "logits")
            for j in range(NTB):
                for k in range(KD):
                    if j == 0:
                        wait_block(2, k)
                    last = mm(b[0:TB, j * NE:(j + 1) * NE], aT[:, k, j * TB:(j + 1) * TB], wr[:, k, :],
                              start=k == 0, stop=k == KD - 1)
            fill_done("logits", last)
            for i in range(6):
                b = to_fill(pe, f"hm{i}")
                for m in range(4):
                    k = 4 * (i % 2) + m
                    last = tr(b[0:TB, m * P:(m + 1) * P], aT[:, k, (i // 2) * TB:(i // 2 + 1) * TB], ident[:])
                fill_done(f"hm{i}", last)
            pe.wait_ge(s["gates"], 1)
            b = to_fill(pe, "gTr")
            for j in range(NTB):
                last = tr(b[0:NE, j * TB:(j + 1) * TB], gates[:, j, :], ident[0:TB, 0:TB])
            fill_done("gTr", last)
            pe.wait_ge(s["consts"], CONSTS + 2)
            b = to_fill(pe, "rank")
            for j in range(NTB):
                for i in range(j + 1):
                    w = before[:] if i == j else ones[0:TB, 0:TB]
                    mm(b[0:TB, j * NE:(j + 1) * NE], w, sel[:, i, :], start=i == 0, stop=i == j)
            for i in range(NTB):
                last = mm(b[:, NTB * NE:(NTB + 1) * NE], ones[0:TB, :], sel[:, i, :], start=i == 0, stop=i == NTB - 1)
            fill_done("rank", last)
            pe.wait_ge(s["bd_loaded"], 16 * 3)
            wait_drained(pe, "gTr")
            for i in range(KD):
                b = to_fill(pe, f"bd{i}")
                fill_done(f"bd{i}", mm(b[:, 0:T], b_down[:, i * P:(i + 1) * P], gatesT[:], start=True, stop=True))
            for i in range(8):
                pe.wait_ge(drained[i], before_experts[i])

            aux = [bank[6], bank[7]]

            def gather(sm, n):
                pe.wait_ge(sm["onehot"], n + 1)
                for h in range(2):
                    for i in range(4):
                        k = 4 * h + i
                        for j in range(NTB):
                            last = mm(aux[h][:, i * CAP:(i + 1) * CAP], hm_tok[0:TB, j, k * P:(k + 1) * P],
                                      onehot[:, j, :], start=j == 0, stop=j == NTB - 1)
                    last.then_inc(sm["gather_filled"], 1)

            def split_product(target, stationary, c, at, start, stop):
                high, low = stationary
                wide = 512
                for x, half in ((high, 0), (high, 1), (low, 0)):
                    for t, b in enumerate(target):
                        w = pair(c, half)[:, at + t * wide:at + (t + 1) * wide]
                        last = mm(b[:], x, w, start=start and x is high and half == 0, stop=stop and x is low)
                return last

            def expert(sm, n, first, last_one):
                pe.wait_ge(sm["x_low"], n * 2 + 2)
                pe.wait_ge(sm["selector"], n + 1)
                if not first:
                    pe.wait_ge(sm["h_low"], n * 2)
                    pe.wait_ge(sm["spread"], n)
                    pe.wait_ge(sm["sc_added"], n * KD - KD)
                for t in range(4):
                    mm(bank[t][:], selector[:], bias[:, t * 512:(t + 1) * 512], start=True, stop=False)
                for c in range(KD):
                    wait_high(pe, sm, n, c)
                    wait_low(pe, sm, n, c)
                    split_product(bank[0:4], (x_high[:, c, :], x_low[:, c, :]), c, 0, False,
                                  c == KD - 1).then_inc(sm["chunk_used"], 1)
                if not last_one:
                    gather(sm, n + 1)
                for h in range(2):
                    pe.wait_ge(sm["hid"], n * 2 + h + 1)
                    for i in range(4):
                        k = 4 * h + i
                        last = tr(bank[h][:, i * P:(i + 1) * P], gbuf[:, k * P:(k + 1) * P], ident[:])
                    last.then_inc(sm["ht_filled"], 1)
                if not first:
                    pe.wait_ge(sm["y_low"], n * 2)
                    pe.wait_ge(sm["spread"], n)
                    scatter(sm, n - 1, 0, 2)
                    if not last_one:
                        pe.wait_ge(sm["x_low"], n * 2 + 4)
                    scatter(sm, n - 1, 2, 6)
                if not first:
                    pe.wait_ge(sm["sc_added"], n * KD - KD + 2)
                for c in range(KD, CHUNKS):
                    if c in (KD, KD + 2):
                        pe.wait_ge(sm["h_low"], n * 2 + (1 if c == KD else 2))
                    wait_high(pe, sm, n, c)
                    wait_low(pe, sm, n, c)
                    for k in range(2):
                        m = 2 * (c - KD) + k
                        last = split_product(bank[4:6], (h_high[:, m, :], h_low[:, m, :]), c, k * D, m == 0, m == KD - 1)
                    last.then_inc(sm["chunk_used"], 1)
                    if c == KD:
                        if not first:
                            pe.wait_ge(sm["sc_added"], n * KD - KD + 4)
                            scatter(sm, n - 1, 6, 8)
                        gated_by_slot(sm, n, first)

            def gated_by_slot(sm, n, first):
                pe.wait_ge(sm["gated"], n + 1)
                if not first:
                    pe.wait_ge(sm["sc_added"], n * KD - KD + 5)
                for j in range(NTB):
                    last = tr(bank[2][0:CAP, j * TB:(j + 1) * TB], gated[:, j, :], ident[0:TB, 0:TB])
                last.then_inc(sm["pt_filled"], 1)

            def scatter(sm, n, i0, i1):
                for i in range(i0, i1):
                    for y in (y_high, y_low):
                        last = mm(bank[SCATTER_BANKS[i]][:, 0:T], y[:, i * P:(i + 1) * P], spread,
                                  start=y is y_high, stop=y is y_low)
                    last.then_inc(sm["sc_filled"], 1)

            def run_experts(sm, base):
                gather(sm, base)
                pe.wait_ge(s["bias_ready"], 1)
                expert(sm, base, True, False)
                with pe.Fori(1, NE - 1) as e:
                    expert(sm, base + e, False, False)
                expert(sm, base + NE - 1, False, True)
                pe.wait_ge(sm["y_low"], (base + NE) * 2)
                pe.wait_ge(sm["spread"], base + NE)
                pe.wait_ge(sm["sc_added"], (base + NE - 1) * KD)
                scatter(sm, base + NE - 1, 0, 6)
                pe.wait_ge(sm["sc_added"], (base + NE - 1) * KD + 4)
                scatter(sm, base + NE - 1, 6, 8)

            run_experts(first, 0)
            most = pe.value_load(flag[0:1, 0:1], min_val=0, max_val=T)
            with pe.If(most > CAP):
                pe.wait_ge(first["sc_added"], 8 * NE)
                with pe.Fori(1, PASSES) as j:
                    pe.wait_ge(more["sc_added"], (j - 1) * (8 * NE))
                    run_experts(more, (j - 1) * NE)

            sum_squares("rms3", 3)
            pe.wait_ge(s["late_loaded"], 16 * 5)
            wp = chunk_view("down", slot_of(4))
            for i in range(KD):
                b = to_fill(pe, f"pg{i}")
                w = chunk_view("in", slot_of(i // 2))
                for k in range(KD):
                    if i == 0:
                        wait_block(3, k)
                    last = mm(b[:, 0:T], w[:, k, P * (i % 2):P * (i % 2) + P], aT[:, k, :], start=k == 0, stop=k == KD - 1)
                fill_done(f"pg{i}", last)
                b = to_fill(pe, f"pp{i}")
                for k in range(2):
                    last = mm(b[:, 0:T], wp[:, k, i * P:(i + 1) * P], pT[:, k, :], start=k == 0, stop=k == 1)
                fill_done(f"pp{i}", last)
            sum_squares("rms4", 4)
            for t in range(3):
                w = P if t < 2 else TS
                for h in range(2):
                    b = to_fill(pe, f"y{t}{h}")
                    for i in range(4):
                        if t == 0:
                            wait_block(4, 4 * h + i)
                        last = tr(b[0:w, i * P:(i + 1) * P], aT[:, 4 * h + i, t * P:t * P + w], ident[:])
                    fill_done(f"y{t}{h}", last)

        @block.scalar
        def _(act):
            tell = Teller(act, s, "act_order")
            A = nc.scalar.activation

            def out_of(instruction, name):
                instruction.then_inc(drain_sem(name), 1)
                wait_drained(act, name)

            def load(dst, src, name):
                act.dma_start(dst, src).then_inc(s[name], 16)

            xp, xsm = a["x_prompt"][0], a["x_sample"].rearrange("b s d -> (b s) d")
            for t in range(2):
                load(xs[:, t, :], xp[t * P:(t + 1) * P, :], "x_loaded")
            load(xs[0:TS, 2, :], xsm, "x_loaded")
            for name, r, n in (("norm_mix", 0, 8), ("norm_ffn", 8, 8), ("norm_ple", 16, 8), ("norm_final", 24, 8),
                               ("conf_dw_b", 32, 4), ("conf_ln_g", 36, 4), ("conf_ln_b", 40, 4), ("gdn_norm", 44, 1)):
                v = a[name] if name == "norm_final" else a[name][0]
                load(stage[r:r + n, 0, :], v.rearrange("(r c) -> r c", c=P), "params_loaded")
            load(stage[0:96, 1, :], a["conv_qkv_w"][0].rearrange("t (r c) -> (t r) c", c=P), "params_loaded")
            load(stage[0:CK * CB, 2, :], a["conf_dw_w"][0].rearrange("t (r c) -> (t r) c", c=P), "params_loaded")
            load(small8[:, 0:1], a["a_log"].rearrange("o h -> h o"), "params_loaded")
            load(small8[:, 1:2], a["dt_bias"].rearrange("o h -> h o"), "params_loaded")
            load(brt[:], a["b_router"][0:1, :].broadcast_to([TB, NE]), "params_loaded")
            load(hist_rows, a["state_qkv_conv"][0].rearrange("b i c -> (b i) c"), "rows_loaded")
            cs = a["state_conf_conv"][0].rearrange("b i c -> (b i) c")
            for i in range(2):
                load(conf_rows[0:120, i, :], cs[120 * i:120 * (i + 1), :], "rows_loaded")
            for t in range(2):
                load(ps_tok[:, t, :], a["p_prompt"][0, 0, t * P:(t + 1) * P, :], "rows_loaded")
            load(ps_tok[0:TS, 2, :], a["p_sample"][0].rearrange("b s c -> (b s) c"), "rows_loaded")
            state_in = a["state_gdn"][0].rearrange("b h k v -> h k b v")
            state_out = out[5][0].rearrange("b h k v -> h k b v")
            for j in range(2):
                load(st[:, j, :, :], state_in[j], f"state_loaded{j}")
            act.dma_start(out[6][0, :, 0:HIST - 1, :], a["state_qkv_conv"][0, :, 1:HIST, :]).then_inc(s["outs"], 16)
            act.dma_start(out[7][0, :, 0:CK - 2, :], a["state_conf_conv"][0, :, 1:CK - 1, :]).then_inc(s["outs"], 16)

            out_of(nc.scalar.copy(par[:], to_drain(act, "par0")[:, 0:45]), "par0")
            b = to_drain(act, "par1")
            for t in range(4):
                i = nc.scalar.copy(wconv[:, t, :].rearrange("p (g k j) -> p k g j", g=4, k=3),
                                   b[:, 24 * t:24 * (t + 1)].rearrange("p (k g j) -> p k g j", k=3, g=4))
                if t == 3:
                    out_of(i, "par1")
            out_of(nc.scalar.copy(wdw[:].rearrange("p t b -> p (t b)"), to_drain(act, "par2")[:, 0:CK * CB]), "par2")
            for t in range(3):
                w = P if t < 2 else TS
                b = to_drain(act, f"x{t}0")
                out_of(nc.scalar.copy(xT[:, 0:4, t * P:t * P + w], b[:, 0:4 * w].rearrange("p (k t) -> p k t", k=4)), f"x{t}0")

            def squares(dst, wait):
                for k in range(KD):
                    wait(k)
                    A(dst[:, k, :], xT[:, k, :], ACT.Square).then_inc(s["squares"], 1)

            def root(dst, name, scale, e=0):
                act.wait_ge(s["consts"], CONSTS)
                b = to_drain(act, name)
                out_of(A(dst, b[:, 0:T], ACT.Sqrt, bias=eps[:, e:e + 1], scale=scale), name)

            def log(dst, name, scale):
                b = to_drain(act, name)
                out_of(A(dst, b[:, 0:T], ACT.Ln, bias=eps[:, 0:1], scale=scale), name)

            for t in range(3):
                wait_drained(act, f"x{t}1")
            squares(aT, lambda k: None)
            root(rstd[:], "rms1", 1.0 / D)
            out_of(nc.scalar.copy(pT[:, :, 0:TP], to_drain(act, "pT")[:].rearrange("p (k t) -> p k t", k=2)), "pT")
            out_of(nc.scalar.copy(pT[:, :, TP:T], to_drain(act, "pTs")[:, 0:2 * TS].rearrange("p (k t) -> p k t", k=2)), "pTs")
            out_of(A(betaT, to_drain(act, "beta")[0:H, 0:T], ACT.Sigmoid), "beta")
            act.wait_ge(s["params_loaded"], 16 * PARAM_DMAS)
            tell(A(small8[:, 2:3], small8[:, 0:1], ACT.Exp), "expa")
            act.wait_ge(s["sp_in"], 1)
            tell(A(tmp8b, tmp8b, ACT.Exp), "e1_ready")
            act.wait_ge(s["gates_in"], 1)
            tell(A(tmp8b, tmp8b, ACT.Ln), "ln_ready")
            out_of(nc.scalar.copy(gbt[:].rearrange("p i h -> p (i h)"), to_drain(act, "gbt")[:, 0:4 * H]), "gbt")
            act.wait_ge(s["esc_in"], 1)
            tell(A(esc[:], esc[:], ACT.Exp), "esc_ready")

            def gdn_step(g, step):
                def name(x):
                    return f"{x}.{g}"

                AT, Dm, DT, M, QKT, kd, vb, dec, kb, kbg, qg, S1, nsq, nstd = work[g % 2]
                vn, osq = M, kb
                if g and step in ("norm", "tokens"):
                    j = 0 if step == "norm" else 1
                    act.wait_ge(s[f"state_stored{j}"], 16 * g)
                    load(st[:, j, :, :], state_in[2 * g + j], f"state_loaded{j}")
                if step == "norm":
                    for i in range(4):
                        log(nstd[:, i, :], name(f"n{i}"), 1.0)
                    tell(A(nstd[:], nstd[:], ACT.Exp, scale=-0.5), "inverse_norms")
                elif step == "onorm":
                    for j in range(2):
                        log(ostd[:, j, :], name(f"on{j}"), 1.0 / P)
                    tell(A(ostd[:], ostd[:], ACT.Exp, scale=-0.5), "inverse_ostd")
                elif step == "bcast":
                    if g:
                        act.wait_ge(s["sscaled"], 2 * g)
                        act.wait_ge(s["os_ready"], 2 * g)
                        act.wait_ge(s["kbg_ready"], 2 * g)
                    for j in range(2):
                        b = to_drain(act, name(f"bcg{j}"))
                        act.wait_ge(s["dec_diff"], 4 * g + 2 * j + 2)
                        out_of(A(eg[:, j, :], b[:, 0:T], ACT.Exp), name(f"bcg{j}"))
                    tell(A(dec[:], dec[:], ACT.Exp), "dec_exp")
                elif step == "tokens":
                    out_of(nc.scalar.copy(Dm[:].rearrange("p i c -> p (i c)"), to_drain(act, name("T1"))), name("T1"))
                elif step[:2] == "tr":
                    out_of(nc.scalar.copy(DT[:].rearrange("p i c -> p (i c)"), to_drain(act, name(step))), name(step))
                elif step in ("vn0", "vn1"):
                    c = int(step[2])
                    b = to_drain(act, name(step))
                    out_of(nc.scalar.copy(vn[:, c:4:2, :], b[:, 0:2 * P].rearrange("p (j v) -> p j v", j=2)), name(step))
                elif step == "s1":
                    b = to_drain(act, name(step))
                    out_of(nc.scalar.copy(S1[:], b[:, 0:2 * P].rearrange("p (j v) -> p j v", j=2)), name(step))
                elif step == "o":
                    b = to_drain(act, name(step))
                    out_of(nc.scalar.copy(oT[:, 2 * g:2 * g + 2, 0:TP], b[:].rearrange("p (j t) -> p j t", j=2)), name(step))
                    wait_drained(act, name("s2"))
                    act.dma_start(out[2][0, 0, 2 * g:2 * g + 2].rearrange("j k v -> k j v"), sfin[:]).then_inc(s["sfin_stored"], 16)
                j = {"tr2": 0, "lt": 1}.get(step)
                if j is not None:
                    h = 2 * g + j
                    wait_drained(act, f"kv0.{h}")
                    wait_drained(act, f"kv1.{h}")
                    act.dma_start(state_out[h], st[:, j, :, :]).then_inc(s[f"state_stored{j}"], 16)

            n_rows = 0
            for kind, n, x in TIMETABLE:
                if kind == "block" and 1 <= n:
                    what, i, _ = BLOCKS[n - 1]
                    name = f"proj{n - 1}"
                    if x == 0:
                        b = to_drain(act, name)
                        if what == "val":
                            if i >= 2:
                                act.wait_ge(s["u_ready"], 2 * (i - 1))
                            out_of(nc.scalar.copy(vals[i % 2], b[:, 0:T]), name)
                        elif what == "sig":
                            if i:
                                act.wait_ge(s["u_ready"], 2 * i)
                            out_of(A(sig, b[:, 0:T], ACT.Sigmoid), name)
                        elif what == "qkv":
                            if i:
                                act.wait_ge(s["conv_ready"], i)
                            else:
                                act.wait_ge(s["consts"], CONSTS)
                            tell(nc.scalar.copy(raw[:, HIST:HIST + TP], b[:, 0:TP]))
                            out_of(nc.scalar.copy(tail[:, i, :], b[:, TP - HIST:T]), name)
                        elif what == "z":
                            if i:
                                wait_drained(act, f"proj{n - 2}")
                            else:
                                act.wait_ge(s["qkv_ready"], 24)
                            tell(A(sig, b[:, 0:T], ACT.Sigmoid), "z_sig")
                        else:
                            dst = gaT if what == "ga" else gbT
                            out_of(A(dst[:, i, :], b[:, 0:T], ACT.Sigmoid), name)
                    elif x == 1 and what == "qkv":
                        act.wait_ge(s["conv_ready"], i + 1)
                        if i == 0:
                            act.wait_ge(s["u_ready"], 8)
                        tell(A(sig[:, 0:TP], acc[:, 0:TP], ACT.Sigmoid), "silu_sig")
                        if i % 6 == 5:
                            act.wait_ge(s["sample_acc"], i // 6 + 1)
                            tell(A(stmp[:], sacc[:], ACT.Sigmoid), "sample_sig")
                elif kind == "gdn":
                    gdn_step(n, x)
                elif kind in ("conf_rows", "tail"):
                    name = f"crow{n}" if kind == "conf_rows" else f"tail{n}"
                    rows = (30 if n == 0 else TS) if kind == "conf_rows" else 11
                    b = to_drain(act, name)
                    if n_rows:
                        act.wait_ge(s["tail_stored"], 16 * n_rows)
                    out_of(nc.scalar.copy(qrow[0:rows, :], b[0:rows, :]), name)
                    c0 = 512 * n
                    if kind == "tail":
                        act.dma_start(out[3][0, 0, :, c0:c0 + 512], qrow[0:HIST, :]).then_inc(s["tail_stored"], 16)
                        act.dma_start(out[6][0, :, HIST - 1, c0:c0 + 512], qrow[HIST:11, :]).then_inc(s["tail_stored"], 16)
                        n_rows += 2
                    elif n == 0:
                        act.dma_start(out[4][0, 0], qrow[0:30, :]).then_inc(s["tail_stored"], 16)
                        n_rows += 1
                    else:
                        act.dma_start(out[7][0, :, CK - 2, :], qrow[0:TS, :]).then_inc(s["tail_stored"], 16)
                        n_rows += 1
                elif kind == "conf_var":
                    root(vals[1], "cvar", 1.0 / CC, 1)
                    act.wait_ge(s["caff"], 1)
                    tell(A(conf_sq, cv[:], ACT.Sigmoid), "csig")

            act.wait_ge(s["mix"], KD)
            act.dma_start(b_down, a["b_down"][0]).then_inc(s["bd_loaded"], 16)
            for i in range(2):
                act.dma_start(b_stage[NE * i:NE * (i + 1), :], a["b_gate_up"][0]).then_inc(s["bd_loaded"], 16)
            squares(zT, lambda k: wait_drained(act, f"wo{k}"))
            root(rstd[:], "rms2", 1.0 / D)
            for i in range(6):
                b = to_drain(act, f"hm{i}")
                out_of(nc.scalar.copy(hm_tok[0:TB, i // 2, (i % 2) * 512:(i % 2 + 1) * 512], b[0:TB, :]), f"hm{i}")

            def make_high(sm, sems, n, c, filled):
                slot = slot_of(c)
                act.wait_ge(sems[slot], n * 32 + 16 * (c // RING + 1 + filled[slot]))
                nc.scalar.copy(pair(c, 0), raw_chunk(c)).then_inc(sm["high"], 1)

            act.wait_ge(s["nmax"], 1)
            for j in range(NTB):
                tell(A(gates[:, j, :], lg[:, j, 0:NE], ACT.Exp, bias=nmax[:, j:j + 1]), "wexp")
            act.wait_ge(s["bd_loaded"], 16 * 3)
            nc.scalar.copy(bias, b_stage).then_inc(s["b_high"], 1)
            out_of(nc.scalar.copy(gatesT, to_drain(act, "gTr")[0:NE, 0:T]), "gTr")

            aux = [bank[6], bank[7]]

            def four(v, h):
                return v[:, 4 * h:4 * h + 4, :].rearrange("p k c -> p (k c)")

            def gathered(sm, n):
                for h in range(2):
                    act.wait_ge(sm["gather_filled"], n * 2 + h + 1)
                    nc.scalar.copy(four(x_high, h), aux[h][:]).then_inc(sm["x_high"], 1)

            def outputs_high(sm, n):
                act.wait_ge(sm["slot_gate"], n + 1)
                for h in range(2):
                    A(y_high[:, 512 * h:512 * (h + 1)], bank[4 + h][:], ACT.Identity,
                      scale=slot_gate[:, 0:1]).then_inc(sm["y_high"], 1)

            def expert(sm, sems, n, filled, first, last_one):
                def high(c, m=n):
                    act.wait_ge(sm["chunk_used"], m * CHUNKS + (c + 1 - PAIRS))
                    make_high(sm, sems, m, c, filled)

                high(3)
                high(4)
                if not first:
                    act.wait_ge(sm["chunk_used"], n * CHUNKS)
                    outputs_high(sm, n - 1)
                for c in range(5, 10):
                    high(c)
                for h in range(2):
                    act.wait_ge(sm["gate_in"], n * 2 + h + 1)
                    A(gsig[:, 512 * h:512 * (h + 1)], gbuf[:, 512 * h:512 * (h + 1)], ACT.Sigmoid,
                      scale=ALPHA).then_inc(sm["gate_sig"], 1)
                high(10)
                if not last_one:
                    gathered(sm, n + 1)
                for h in range(2):
                    act.wait_ge(sm["ht_filled"], n * 2 + h + 1)
                    nc.scalar.copy(four(h_high, h), bank[h][:]).then_inc(sm["h_high"], 1)
                high(11)
                if not last_one:
                    for c in range(PAIRS):
                        high(c, n + 1)

            def run_experts(sm, sems, base, filled):
                for c in range(PAIRS):
                    make_high(sm, sems, base, c, filled)
                gathered(sm, base)
                expert(sm, sems, base, filled, True, False)
                with act.Fori(1, NE - 1) as e:
                    expert(sm, sems, base + e, filled, False, False)
                expert(sm, sems, base + NE - 1, filled, False, True)
                act.wait_ge(sm["chunk_used"], (base + NE) * CHUNKS)
                outputs_high(sm, base + NE - 1)

            run_experts(first, loaded, 0, slot_fills)
            most = act.value_load(flag[0:1, 0:1], min_val=0, max_val=T)
            with act.If(most > CAP):
                act.wait_ge(first["sc_added"], NE * KD)
                with act.Fori(1, PASSES) as j:
                    act.wait_ge(more["sc_added"], (j - 1) * (NE * KD))
                    run_experts(more, more_loaded, (j - 1) * NE, [0] * RING)
                act.wait_ge(more["sc_added"], (PASSES - 1) * NE * KD)

            squares(zT, lambda k: act.wait_ge(first["sc_added"], NE * KD - KD + k + 1))
            root(rstd[:], "rms3", 1.0 / D)
            for i in range(KD):
                b = to_drain(act, f"pg{i}")
                if i >= 2:
                    act.wait_ge(s["x3"], i - 1)
                out_of(A(pieces[:, i % 2, :], b[:, 0:T], ACT.Sigmoid), f"pg{i}")
            squares(zT, lambda k: act.wait_ge(s["x3"], k + 1))
            root(rstd[:], "rms4", 1.0 / D)
            for t in range(3):
                w = P if t < 2 else TS
                for h in range(2):
                    name = f"y{t}{h}"
                    b = to_drain(act, name)
                    out_of(nc.scalar.copy(yrows[0:w, t, 512 * h:512 * (h + 1)], b[0:w, :]), name)
                    dst = out[0][0, t * P:(t + 1) * P, :] if t < 2 else out[1].rearrange("b s d -> (b s) d")
                    act.dma_start(dst[:, 512 * h:512 * (h + 1)], yrows[0:w, t, 512 * h:512 * (h + 1)]).then_inc(s["outs"], 16)
            act.wait_ge(s["outs"], 16 * 8)
            act.wait_ge(s["tail_stored"], 16 * n_rows)
            act.wait_ge(s["sfin_stored"], 16 * 4)
            for j in range(2):
                act.wait_ge(s[f"state_stored{j}"], 16 * 4)

        @block.vector
        def _(dve):
            v = nc.vector
            tell = Teller(dve, s, "dve_order")

            def out_of(instruction, name):
                instruction.then_inc(drain_sem(name), 1)
                wait_drained(dve, name)

            for t in range(3):
                w = P if t < 2 else TS
                b = to_drain(dve, f"x{t}1")
                out_of(v.tensor_copy(xT[:, 4:8, t * P:t * P + w], b[:, 0:4 * w].rearrange("p (k t) -> p k t", k=4)), f"x{t}1")

            def norm(name, gain):
                wait_drained(dve, name)
                tell(v.reciprocal(rstd[:], rstd[:]))
                for k in range(KD):
                    i = v.scalar_tensor_tensor(aT[:, k, :], xT[:, k, :], par[:, gain + k:gain + k + 1], rstd[:], ALU.mult, ALU.mult)
                    i.then_inc(s["aT_ready"], 1)

            wait_drained(dve, "par0")
            norm("rms1", 0)
            for i in range(2):
                b = to_drain(dve, f"hist{i}")
                n = 12 * TS * HIST
                out_of(v.tensor_copy(hist[:, 12 * i:12 * (i + 1), :].rearrange("p m r -> p (m r)"), b[:, 0:n]), f"hist{i}")
            for i in range(2):
                b = to_drain(dve, f"ch{i}")
                for m in range(CB):
                    c = v.tensor_copy(us[:, m, 4 * i:4 * i + 4, 0:CK - 1], b[:, 120 * m:120 * (m + 1)].rearrange("p (b t) -> p b t", b=4))
                    if m == CB - 1:
                        out_of(c, f"ch{i}")
            b = to_drain(dve, "a")
            dve.wait_ge(s["params_loaded"], 16 * PARAM_DMAS)
            out_of(v.tensor_scalar(tmp8, b[0:H, 0:T], small8[:, 1:2], None, ALU.add), "a")
            tell(v.tensor_scalar(tmp8b, tmp8, -1.0, None, ALU.mult))
            tell(v.tensor_tensor(tmp8b, tmp8b, tmp8, ALU.min), "sp_in")
            dve.wait_ge(s["e1_ready"], 1)
            tell(v.tensor_scalar(tmp8b, tmp8b, 1.0, None, ALU.add), "gates_in")
            dve.wait_ge(s["ln_ready"], 1)
            tell(v.scalar_tensor_tensor(tmp8, tmp8, 0.0, tmp8b, ALU.max, ALU.add))
            dve.wait_ge(s["expa"], 1)
            tell(v.tensor_scalar(gT, tmp8, small8[:, 2:3], -1.0, ALU.mult, ALU.mult), "gT_ready")
            tell(v.tensor_copy(gcF[:, TP:T], gT[:, TP:T]), "gcF_ready")
            b = to_drain(dve, "gct")
            out_of(v.tensor_copy(gct[:].rearrange("p i h -> p (i h)"), b[:, 0:4 * H]), "gct")
            tell(v.tensor_tensor(esc[:, 0:2, :], gct[:, 2:4, :], gct[:, 0:2, :], ALU.subtract))
            tell(v.tensor_copy(esc[:, 2:4, :], gct[:, 2:4, :]), "esc_in")
            b = to_drain(dve, "gcf")
            out_of(v.tensor_copy(gcF[:, 0:TP], b[0:H, 0:TP]), "gcf")

            def four(x):
                return x[:].rearrange("p i c -> p (i c)")

            def bank4(b):
                return b[:].rearrange("p (i c) -> p i c", i=4)

            def each4(x):
                return x.unsqueeze(1).broadcast_to([P, 4, P])

            def gdn_step(g, step):
                def name(x):
                    return f"{x}.{g}"

                AT, Dm, DT, M, QKT, kd, vb, dec, kb, kbg, qg, S1, nsq, nstd = work[g % 2]
                vn, osq = M, kb
                q2, k2 = qkvT[:, 6 * g:6 * g + 2, :], qkvT[:, 6 * g + 2:6 * g + 4, :]
                if step == "norm":
                    if g >= 2:
                        wait_drained(dve, f"o.{g - 2}")
                    dve.wait_ge(s["inverse_norms"], g + 1)
                    tell(v.scalar_tensor_tensor(q2, q2, float(P) ** -0.5, nstd[:, 0:2, :], ALU.mult, ALU.mult), "nrm")
                    tell(v.tensor_tensor(k2, k2, nstd[:, 2:4, :], ALU.mult), "nrm")
                    tell(v.tensor_copy(kq[:, :, :, 0], k2[:, :, TP:T]))
                    tell(v.tensor_copy(kq[:, :, :, 1], q2[:, :, TP:T]))
                    tell(v.tensor_tensor(qk_s[:], k2[:, :, TP:T], q2[:, :, TP:T], ALU.mult), "kq_ready")
                elif step == "bcast":
                    for j in range(2):
                        h = 2 * g + j
                        b = to_drain(dve, name(f"bcg{j}"))
                        for c in range(2):
                            tell(v.tensor_scalar(dec[:, 2 * j + c, :], chunk(b, c), gct[:, c, h:h + 1], 0.0,
                                                 ALU.subtract, ALU.min), "dec_diff")
                        b = to_drain(dve, name(f"bcb{j}"))
                        tell(v.tensor_tensor(kb[:, j, :], k_of(g, j), b[:, 0:T], ALU.mult), "kb_ready")
                        out_of(v.tensor_copy(beta_s[:, j, :], b[:, TP:T]), name(f"bcb{j}"))
                    dve.wait_ge(s["dec_exp"], g + 1)
                    tell(v.tensor_tensor(dec[:], dec[:], each4(causal[:]), ALU.mult))
                elif step == "scores":
                    b = to_drain(dve, name("AT"))
                    out_of(v.tensor_tensor(four(AT), b[:], four(dec), ALU.mult), name("AT"))
                    dve.wait_ge(s["masks_ready"], 1)
                    b = to_drain(dve, name("QK"))
                    out_of(v.tensor_tensor(four(QKT), b[:], four(dec), ALU.mult), name("QK"))
                    tell(v.tensor_tensor(DT[:], AT[:], each4(neg_first[:]), ALU.mult))
                    tell(v.tensor_tensor(DT[:], DT[:], each4(ident[:]), ALU.add), "DT0_ready")
                elif step == "tokens":
                    dve.wait_ge(s["esc_ready"], 1)
                    wait_drained(dve, "gbt")
                    for job, dst, col in (("kt", kd, esc[:, 0:2, :]), ("vt", vb, gbt[:, 2:4, :])):
                        b = to_drain(dve, name(job))
                        for i in range(4):
                            h = 2 * g + i // 2
                            x = v.tensor_scalar(dst[:, i, :], b[:, i * P:(i + 1) * P], col[:, i % 2, h:h + 1], None, ALU.mult)
                            if i == 3:
                                out_of(x, name(job))
                            else:
                                tell(x)
                elif step[:2] == "ad":
                    lv = len(LEVELS) if step == "adl" else int(step[2])
                    b = to_drain(dve, name(step))
                    out_of(v.tensor_tensor(M[:], bank4(b), each4(neg_mask[:, lv, :]), ALU.mult), name(step))
                elif step[:2] == "dm":
                    b = to_drain(dve, name(step))
                    out_of(v.tensor_tensor(four(Dm), four(Dm), b[:], ALU.add), name(step))
                elif step == "lt":
                    b = to_drain(dve, name(step))
                    out_of(v.tensor_tensor(four(DT), four(DT), b[:], ALU.add), name(step))
                elif step == "ks":
                    b = to_drain(dve, name(step))
                    out_of(v.tensor_tensor(vb[:, 1:4:2, :], vb[:, 1:4:2, :], b[:, 0:2 * P].rearrange("p (j v) -> p j v", j=2),
                                           ALU.subtract), name(step))
                elif step == "s2":
                    b = to_drain(dve, name(step))
                    if g:
                        dve.wait_ge(s["sfin_stored"], 16 * g)
                    for j in range(2):
                        h = 2 * g + j
                        x = v.scalar_tensor_tensor(sfin[:, j, :], S1[:, j, :], esc[:, 3, h:h + 1], b[:, j * P:(j + 1) * P],
                                                   ALU.mult, ALU.add)
                        if j:
                            out_of(x, name(step))
                        else:
                            tell(x)
                elif step == "onorm":
                    dve.wait_ge(s["inverse_ostd"], g + 1)
                    o2 = oT[:, 2 * g:2 * g + 2, :]
                    tell(v.scalar_tensor_tensor(o2, o2, par[:, 44:45], ostd[:], ALU.mult, ALU.mult), "onorm_ready")
                if step in SAMPLE_STEPS:
                    sample_step(g, *SAMPLE_STEPS[step])

            def sample_step(g, step, j):
                h = 2 * g + j
                if step == "skq":
                    b = to_drain(dve, f"skq.{h}")
                    wait_drained(dve, f"bcg{j}.{g}")
                    kv = b[:, 0:2 * TS].rearrange("p (i x) -> p i x", x=2)
                    e = eg[:, j, TP:T]
                    tell(v.tensor_tensor(sv[:, 0, :], kv[:, :, 0], e, ALU.mult))
                    tell(v.tensor_tensor(sv[:, 1, :], kv[:, :, 1], e, ALU.mult))
                    out_of(v.tensor_copy(sv[:, 3, :], b[:, 16:24]), f"skq.{h}")
                    tell(v.tensor_tensor(sv[:, 0, :], v_of(g, j)[:, TP:T], sv[:, 0, :], ALU.subtract))
                    tell(v.tensor_tensor(sv[:, 2, :], sv[:, 0, :], beta_s[:, j, :], ALU.mult), "svn_ready")
                    tell(v.tensor_tensor(sv[:, 3, :], sv[:, 3, :], sv[:, 2, :], ALU.mult))
                    tell(v.tensor_tensor(oT[:, h, TP:T], sv[:, 1, :], sv[:, 3, :], ALU.add), "os_ready")
                elif step == "srow":
                    b = to_drain(dve, f"srow.{h}")
                    tell(v.tensor_copy(krow[:], b[0:TS, 0:P]))
                    out_of(v.tensor_tensor(vbd[:], b[0:TS, P:2 * P].unsqueeze(1).broadcast_to([TS, TS, P]),
                                           ident[0:TS, 0:TS].unsqueeze(2).broadcast_to([TS, TS, P]), ALU.mult), f"srow.{h}")
                else:
                    dve.wait_ge(s["sscaled"], h + 1)
                    for i in range(2):
                        b = to_drain(dve, f"kv{i}.{h}")
                        x = st[:, j, 4 * i:4 * i + 4, :]
                        out_of(v.tensor_tensor(x, x, b[:].rearrange("p (i v) -> p i v", i=4), ALU.add), f"kv{i}.{h}")

            def conv_block(i):
                wait_drained(dve, f"proj{8 + i}")
                x = acc[:, 0:TP]
                tell(v.tensor_scalar(x, raw[:, 0:TP], wconv[:, 0, i:i + 1], None, ALU.mult))
                for t in range(1, 4):
                    tell(v.scalar_tensor_tensor(x, raw[:, t:t + TP], wconv[:, t, i:i + 1], x, ALU.mult, ALU.add),
                         "conv_ready" if t == 3 else None)
                if i % 6 == 5:
                    b = slice(i - 5, i + 1)
                    hh = hist[:, b, :].rearrange("p m (b t) -> p m b t", t=HIST)

                    def w(t):
                        return wconv[:, t, b].unsqueeze(2).broadcast_to([P, 6, TS])

                    tell(v.tensor_tensor(sacc[:], hh[:, :, :, 0], w(0), ALU.mult))
                    for t in range(1, 4):
                        src = hh[:, :, :, t] if t < 3 else tail[:, b, HIST:11]
                        tell(v.tensor_tensor(stmp[:], src, w(t), ALU.mult))
                        tell(v.tensor_tensor(sacc[:], sacc[:], stmp[:], ALU.add), "sample_acc" if t == 3 else None)

            def conf_taps(first_tap, n):
                for t in range(first_tap, min(first_tap + n, CK * CB)):
                    i, tap = divmod(t, CK)
                    x, w = cv[:, i, 0:TP], wdw[:, tap, i:i + 1]
                    if tap == 0:
                        tell(v.tensor_scalar(x, up[:, i, 0:TP], w, par[:, 32 + i:33 + i], ALU.mult, ALU.add))
                        p = vals[0][:, 0:TS * CK].rearrange("p (b t) -> p b t", b=TS)
                        tell(v.tensor_tensor(p, us[:, i, :, :], wdw[:, :, i].unsqueeze(1).broadcast_to([P, TS, CK]), ALU.mult))
                        tell(v.tensor_reduce(cv[:, i, TP:T], p, AX.X, ALU.add))
                        tell(v.tensor_scalar(cv[:, i, TP:T], cv[:, i, TP:T], par[:, 32 + i:33 + i], None, ALU.add))
                    else:
                        tell(v.scalar_tensor_tensor(x, up[:, i, tap:tap + TP], w, x, ALU.mult, ALU.add),
                             "conf_done" if t == CK * CB - 1 else None)

            def over_blocks(x):
                return x.unsqueeze(1).broadcast_to([P, CB, T])

            for kind, n, x in TIMETABLE:
                if kind == "block" and n:
                    what, i, _ = BLOCKS[n - 1]
                    name = f"proj{n - 1}"
                    if x == 0 and what == "sig":
                        wait_drained(dve, name)
                        wait_drained(dve, f"proj{n - 3}")
                        if i == 0:
                            dve.wait_ge(s["consts"], CONSTS)
                        tell(v.tensor_tensor(up[:, i, 30:286], vals[i % 2][:, 0:TP], sig[:, 0:TP], ALU.mult), "u_ready")
                        tell(v.tensor_tensor(us[:, i, :, CK - 1], vals[i % 2][:, TP:T], sig[:, TP:T], ALU.mult), "u_ready")
                    elif x == 0 and what == "qkv":
                        if i == 0:
                            wait_drained(dve, "par1")
                            wait_drained(dve, "par2")
                        conv_block(i)
                    elif x == 0 and what == "z":
                        dve.wait_ge(s["z_sig"], i + 1)
                        out_of(v.tensor_tensor(zT[:, i, :], bank[uses[name][0]][:, 0:T], sig, ALU.mult), name)
                    elif x == 2 and what == "qkv":
                        dve.wait_ge(s["silu_sig"], i + 1)
                        tell(v.tensor_tensor(qkvT[:, i, 0:TP], acc[:, 0:TP], sig[:, 0:TP], ALU.mult), "qkv_ready")
                        if i % 6 == 5:
                            dve.wait_ge(s["sample_sig"], i // 6 + 1)
                            tell(v.tensor_tensor(qkvT[:, i - 5:i + 1, TP:T], sacc[:], stmp[:], ALU.mult), "sample_ready")
                elif kind == "gdn":
                    gdn_step(n, x)
                elif kind == "conf_tap" and (n, x) in CONF_SLOTS:
                    conf_taps(CONF_SLOTS.index((n, x)), CONF_SLOTS.count((n, x)))
                elif kind == "conf_mean":
                    b = to_drain(dve, "cmu")
                    out_of(v.tensor_scalar(vals[0], b[:, 0:T], 1.0 / CC, None, ALU.mult), "cmu")
                    tell(v.tensor_tensor(cv[:], cv[:], over_blocks(vals[0]), ALU.subtract))
                    tell(v.tensor_tensor(conf_sq, cv[:], cv[:], ALU.mult), "csq")
                elif kind == "conf_var":
                    wait_drained(dve, "cvar")
                    tell(v.reciprocal(vals[1], vals[1]))
                    tell(v.tensor_tensor(cv[:], cv[:], over_blocks(vals[1]), ALU.mult))
                    for i in range(CB):
                        tell(v.tensor_scalar(cv[:, i, :], cv[:, i, :], par[:, 36 + i:37 + i], par[:, 40 + i:41 + i],
                                             ALU.mult, ALU.add), "caff" if i == CB - 1 else None)
                    dve.wait_ge(s["csig"], 1)
                    tell(v.tensor_tensor(cv[:], cv[:], conf_sq, ALU.mult), "cv_ready")

            tell(v.tensor_tensor(oT[:], oT[:], zT, ALU.mult), "onorm_ready")
            wait_drained(dve, f"proj{N_BLOCKS - 1}")
            wait_drained(dve, f"proj{N_BLOCKS - 2}")
            for i in range(KD):
                b = to_drain(dve, f"bb{i}")
                out_of(v.tensor_tensor(gbT[:, i, :], gbT[:, i, :], b[:, 0:T], ALU.mult), f"bb{i}")
            for i in range(KD):
                b = to_drain(dve, f"ba{i}")
                out_of(v.tensor_tensor(gaT[:, i, :], gaT[:, i, :], b[:, 0:T], ALU.mult), f"ba{i}")
                tell(v.tensor_tensor(aT[:, i, :], gaT[:, i, :], gbT[:, i, :], ALU.add), "mix")
            for i in range(KD):
                b = to_drain(dve, f"wo{i}")
                out_of(v.tensor_tensor(xT[:, i, :], xT[:, i, :], b[:, 0:T], ALU.add), f"wo{i}")
            norm("rms2", 8)

            for j in range(2):
                dve.wait_ge(s[f"state_stored{j}"], 16 * 4)
            b = to_drain(dve, "logits")
            for j in range(NTB):
                x = v.tensor_tensor(lg[:, j, 0:NE], b[0:TB, j * NE:(j + 1) * NE], brt[:], ALU.add)
                if j == NTB - 1:
                    out_of(x, "logits")
                else:
                    tell(x)
            tell(v.memset(lg[:, :, NE:NE + TOPK], BIG))
            for j in range(NTB):
                tell(v.max(m8[:, j, :], lg[:, j, 0:NE]))
            tell(v.tensor_scalar(nmax[:], m8[:, :, 0], -1.0, None, ALU.mult), "nmax")
            tell(v.memset(m8[:, :, TOPK:8], BIG))
            for j in range(NTB):
                tell(v.match_replace(rep[:, j, :], m8[:, j, :], lg[:, j, :], -BIG))
            tell(v.tensor_tensor(sel[:], rep[:, :, 0:NE], lg[:, :, 0:NE], ALU.not_equal), "selected")
            dve.wait_ge(s["wexp"], NTB)
            tell(v.tensor_tensor(gates[:], gates[:], sel[:], ALU.mult))
            tell(v.tensor_reduce(wsum[:], gates[:], AX.X, ALU.add))
            tell(v.reciprocal(wsum[:], wsum[:]))
            tell(v.tensor_tensor(gates[:], gates[:], wsum[:].unsqueeze(2).broadcast_to([TB, NTB, NE]), ALU.mult), "gates")
            b = to_drain(dve, "rank")
            r0 = rank[:, :, 0:NE]
            far = 10000.0
            tell(v.scalar_tensor_tensor(r0, b[0:TB, 0:NTB * NE].rearrange("p (j e) -> p j e", j=NTB), far, sel[:],
                                        ALU.add, ALU.mult))
            out_of(v.tensor_copy(cnt[:], b[:, NTB * NE:(NTB + 1) * NE]), "rank")
            tell(v.tensor_scalar(r0, r0, far, None, ALU.subtract))
            for j in range(1, PASSES):
                tell(v.tensor_scalar(rank[:, :, j * NE:(j + 1) * NE], r0, float(CAP * j), None, ALU.subtract))
            tell(v.tensor_reduce(cmax, cnt[:], AX.X, ALU.max))
            tell(v.tensor_copy(flag[:], cmax[0:1, :]), "flag_ready")
            PER = 4
            def half(x, h):
                return x[:, 512 * h:512 * (h + 1)]

            def four(x, h):
                return x[:, 4 * h:4 * h + 4, :].rearrange("p k c -> p (k c)")

            def low_part(sm, n, c):
                wait_high(dve, sm, n, c)
                w = CHUNK_COLS - (GPS_COLS if c < KD else 0)
                v.tensor_tensor(pair(c, 1)[:, 0:w], raw_chunk(c)[:, 0:w], pair(c, 0)[:, 0:w].bitcast(FP32),
                                ALU.subtract).then_inc(sm["low_dve"], 1)

            def x_low_part(sm, n):
                for h in range(2):
                    dve.wait_ge(sm["x_high"], n * 2 + h + 1)
                    v.tensor_tensor(four(x_low, h), bank[6 + h][:], four(x_high, h).bitcast(FP32),
                                    ALU.subtract).then_inc(sm["x_low"], 1)

            def make_selector(sm, e):
                v.tensor_copy(selector[:], eye2[:, bass.ds(e, 1)].broadcast_to([2 * NE, CAP])).then_inc(sm["selector"], 1)

            def make_onehot(sm, n, r):
                x = v.tensor_tensor(onehot[:], iota.unsqueeze(1).broadcast_to([TB, NTB, CAP]),
                                    rank[:, :, bass.ds(r, 1)].broadcast_to([TB, NTB, CAP]), ALU.is_equal)
                x.then_inc(sm["onehot"], 1)
                dve.wait_ge(sm["onehot"], n + 1)

            def expert(sm, n, e, r, first, last_one):
                own = [0]

                def then(x, wait=True):
                    own[0] += 1
                    x.then_inc(sm["dve_e"], 1)
                    if wait:
                        dve.wait_ge(sm["dve_e"], n * PER + own[0])

                low_part(sm, n, 3)
                if not first:
                    dve.wait_ge(sm["pt_filled"], n)
                x = v.tensor_tensor(gated[:], onehot[:], gates[:, :, bass.ds(e, 1)].broadcast_to([TB, NTB, CAP]), ALU.mult)
                x.then_inc(sm["gated"], 1)
                if not last_one:
                    dve.wait_ge(sm["gated"], n + 1)
                    dve.wait_ge(sm["gather_filled"], n * 2 + 2)
                    make_onehot(sm, n + 1, r + 1)
                    dve.wait_ge(sm["chunk_used"], n * CHUNKS + 1)
                    make_selector(sm, e + 1)
                for c in range(4, KD):
                    low_part(sm, n, c)
                    if c == 5 and not first:
                        outputs_low(sm, n - 1)
                dve.wait_ge(sm["chunk_used"], n * CHUNKS + KD)
                for h in range(2):
                    v.tensor_scalar(half(gbuf, h), bank[h][:], LIMIT, None, ALU.min).then_inc(sm["gate_in"], 1)
                for h in range(2):
                    then(v.tensor_scalar(half(ubuf, h), bank[2 + h][:], LIMIT, -LIMIT, ALU.min, ALU.max), h == 1)
                for h in range(2):
                    dve.wait_ge(sm["gate_sig"], n * 2 + h + 1)
                    then(v.tensor_tensor(half(gsig, h), half(gsig, h), half(gbuf, h), ALU.mult))
                    v.scalar_tensor_tensor(half(gbuf, h), half(ubuf, h), 1.0, half(gsig, h), ALU.add,
                                           ALU.mult).then_inc(sm["hid"], 1)
                assert own[0] == PER
                if not last_one:
                    x_low_part(sm, n + 1)
                if not first:
                    add_back(sm, n - 1, 0, 2)
                for h in range(2):
                    dve.wait_ge(sm["h_high"], n * 2 + h + 1)
                    v.tensor_tensor(four(h_low, h), bank[h][:], four(h_high, h).bitcast(FP32),
                                    ALU.subtract).then_inc(sm["h_low"], 1)
                if not first:
                    add_back(sm, n - 1, 2, 6)
                low_part(sm, n, 11)
                if not first:
                    add_back(sm, n - 1, 6, 8)
                dve.wait_ge(sm["pt_filled"], n + 1)
                v.tensor_reduce(slot_gate[:], bank[2][0:CAP, 0:T], AX.X, ALU.add).then_inc(sm["slot_gate"], 1)
                v.tensor_scalar(spread, bank[2][0:CAP, 0:T], 0.0, None, ALU.not_equal).then_inc(sm["spread"], 1)
                if not last_one:
                    for c in range(PAIRS):
                        low_part(sm, n + 1, c)

            def outputs_low(sm, n):
                dve.wait_ge(sm["slot_gate"], n + 1)
                for h in range(2):
                    dve.wait_ge(sm["y_high"], n * 2 + h + 1)
                    v.scalar_tensor_tensor(half(y_low, h), bank[4 + h][:], slot_gate[:, 0:1], half(y_high, h).bitcast(FP32),
                                           ALU.mult, ALU.subtract).then_inc(sm["y_low"], 1)

            def add_back(sm, n, i0, i1):
                for i in range(i0, i1):
                    dve.wait_ge(sm["sc_filled"], n * KD + (i + 1))
                    v.tensor_tensor(xT[:, i, :], xT[:, i, :], bank[SCATTER_BANKS[i]][:, 0:T], ALU.add).then_inc(sm["sc_added"], 1)

            def run_experts(sm, base, r0):
                for c in range(PAIRS):
                    low_part(sm, base, c)
                x_low_part(sm, base)
                expert(sm, base, 0, r0, True, False)
                with dve.Fori(1, NE - 1) as e:
                    expert(sm, base + e, e, r0 + e, False, False)
                expert(sm, base + NE - 1, NE - 1, r0 + NE - 1, False, True)
                outputs_low(sm, base + NE - 1)
                add_back(sm, base + NE - 1, 0, KD)

            dve.wait_ge(s["consts"], CONSTS + 2)
            make_onehot(first, 0, 0)
            make_selector(first, 0)
            for i in range(KD):
                b = to_drain(dve, f"bd{i}")
                out_of(v.tensor_tensor(xT[:, i, :], xT[:, i, :], b[:, 0:T], ALU.add), f"bd{i}")
            dve.wait_ge(s["b_high"], 1)
            low_rows = slice(NE, 2 * NE)
            tell(v.tensor_tensor(bias[low_rows], b_stage[low_rows], bias[low_rows].bitcast(FP32), ALU.subtract), "bias_ready")
            run_experts(first, 0, 0)
            most = dve.value_load(flag[0:1, 0:1], min_val=0, max_val=T)
            with dve.If(most > CAP):
                dve.wait_ge(first["sc_added"], NE * KD)
                with dve.Fori(1, PASSES) as j:
                    dve.wait_ge(more["sc_added"], (j - 1) * (NE * KD))
                    make_onehot(more, (j - 1) * NE, j * NE)
                    make_selector(more, 0)
                    run_experts(more, (j - 1) * NE, j * NE)
                dve.wait_ge(more["sc_added"], (PASSES - 1) * NE * KD)
            dve.wait_ge(first["sc_added"], NE * KD)

            norm("rms3", 16)
            for i in range(KD):
                wait_drained(dve, f"pg{i}")
                b = to_drain(dve, f"pp{i}")
                x = pieces[:, i % 2, :]
                out_of(v.tensor_tensor(x, x, b[:, 0:T], ALU.mult), f"pp{i}")
                tell(v.tensor_tensor(xT[:, i, :], xT[:, i, :], x, ALU.add), "x3")
            norm("rms4", 24)

        @block.gpsimd
        def _(pool):
            g_ = nc.gpsimd
            tell = Teller(pool, s, "pool_order")
            tell(g_.memset(ident[:], 0.0))
            tell(g_.affine_select(out=ident[:], in_=ident[:], compare_op=ALU.not_equal, fill=1.0, base=0,
                                  pattern=[[-1, P]], channel_multiplier=1))
            tell(g_.memset(ones[:], 1.0))
            tell(g_.affine_select(out=causal[:], in_=ones[:], compare_op=ALU.is_ge, fill=0.0, base=0,
                                  pattern=[[1, P]], channel_multiplier=-1), "consts")
            tell(g_.tensor_copy(sel8[:], ident[0:H, 0:H].unsqueeze(2).broadcast_to([H, H, P])), "consts")
            for i in range(2):
                r = slice(NE * i, NE * (i + 1))
                tell(g_.tensor_copy(eye2[r, :], ident[r, r]))
            tell(g_.memset(raw[:, 0:HIST], 0.0))
            tell(g_.memset(eps[:, 0:1], NORM_EPS))
            tell(g_.memset(eps[:, 1:2], LN_EPS))
            tell(g_.memset(up[:, :, 0:CK - 1], 0.0), "consts")

            tell(g_.memset(neg_first[:], 0.0))
            x = neg_first[:].rearrange("p (a b) -> p a b", b=2)[:, :, 1]
            tell(g_.affine_select(out=x, in_=x, compare_op=ALU.not_equal, fill=-1.0, base=0,
                                  pattern=[[-2, P // 2]], channel_multiplier=1))
            tell(g_.memset(neg_mask[:], 0.0))
            for lv, side in enumerate(LEVELS + [P // 2]):
                n = P // (2 * side)
                x = neg_mask[:, lv, :].rearrange("p (a b i) -> p a b i", a=n, b=2)[:, :, 0, :]
                tell(g_.memset(x, -1.0))
                tell(g_.affine_select(out=x, in_=x, compare_op=ALU.is_ge, fill=0.0, base=-side,
                                      pattern=[[-2 * side, n], [0, side]], channel_multiplier=1))
                tell(g_.affine_select(out=x, in_=x, compare_op=ALU.is_ge, fill=0.0, base=2 * side - 1,
                                      pattern=[[2 * side, n], [0, side]], channel_multiplier=-1),
                     "masks_ready" if lv == len(LEVELS) else None)

            def gdn_step(g, step):
                AT, Dm, DT, M, QKT, kd, vb, dec, kb, kbg, qg, S1, nsq, nstd = work[g % 2]
                vn, osq = M, kb
                qk4 = qkvT[:, 6 * g:6 * g + 4, :]
                if step == "norm":
                    pool.wait_ge(s["qkv_ready"], 6 * (g + 1))
                    pool.wait_ge(s["sample_ready"], g + 1)
                    if g >= 2:
                        wait_drained(pool, f"o.{g - 2}")
                        wait_drained(pool, f"s2.{g - 2}")
                        for j in range(2):
                            to_drain(pool, f"on{j}.{g - 2}")
                    tell(g_.tensor_tensor(nsq[:], qk4, qk4, ALU.mult), "nsq")
                elif step == "bcast":
                    pool.wait_ge(s["kb_ready"], 2 * (g + 1))
                    for j in range(2):
                        wait_drained(pool, f"bcg{j}.{g}")
                    tell(g_.tensor_tensor(kbg[:], kb[:], eg[:], ALU.mult), "kbg_ready")
                    tell(g_.tensor_tensor(qg[:], qkvT[:, 6 * g:6 * g + 2, :], eg[:], ALU.mult), "kbg_ready")
                elif step == "onorm":
                    wait_drained(pool, f"o.{g}")
                    pool.wait_ge(s["os_ready"], 2 * (g + 1))
                    o2 = oT[:, 2 * g:2 * g + 2, :]
                    tell(g_.tensor_tensor(osq[:], o2, o2, ALU.mult), "osq_ready")
                if SAMPLE_STEPS.get(step, ("", 0))[0] == "skq":
                    j = SAMPLE_STEPS[step][1]
                    to_drain(pool, f"skq.{2 * g + j}")
                    x = st[:, j, :, :]
                    tell(g_.tensor_tensor(x, x, eg[:, j, TP:T].unsqueeze(2).broadcast_to([P, TS, P]), ALU.mult), "sscaled")

            for kind, n, x in TIMETABLE:
                if kind == "gdn":
                    gdn_step(n, x)
            for j in range(2):
                pool.wait_ge(s[f"state_stored{j}"], 16 * 4)
            tell(g_.iota(iota_int, pattern=[[1, CAP]], base=0, channel_multiplier=0))
            tell(g_.tensor_copy(iota, iota_int), "consts")
            tell(g_.affine_select(out=before, in_=ones[0:TB, 0:TB], compare_op=ALU.is_ge, fill=0.0, base=-1,
                                  pattern=[[1, TB]], channel_multiplier=-1), "consts")

            def low_part(sm, n, c):
                wait_high(pool, sm, n, c)
                at = CHUNK_COLS - GPS_COLS if c < KD else 0
                g_.tensor_tensor(pair(c, 1)[:, at:], raw_chunk(c)[:, at:], pair(c, 0)[:, at:].bitcast(FP32),
                                 ALU.subtract).then_inc(sm["low_gps"], 1)

            def run_experts(sm, base):
                for c in range(CHUNKS - 1):
                    low_part(sm, base, c)
                with pool.Fori(1, NE) as e:
                    for c in range(CHUNKS - 1):
                        low_part(sm, base + e, c)

            run_experts(first, 0)
            pool.wait_ge(s["flag_ready"], 1)
            most = pool.value_load(flag[0:1, 0:1], min_val=0, max_val=T)
            with pool.If(most > CAP):
                with pool.Fori(1, PASSES) as j:
                    run_experts(more, (j - 1) * NE)


_INS = ["x_prompt", "x_sample", "p_prompt", "p_sample", "state_gdn", "state_qkv_conv", "state_conf_conv",
        "norm_mix", "w_in", "conv_qkv_w", "a_log", "dt_bias", "gdn_norm", "w_gdn_out", "conf_dw_w", "conf_dw_b",
        "conf_ln_g", "conf_ln_b", "w_conf_out", "w_out", "norm_ffn", "w_router", "b_router", "w_gate_up", "b_gate_up",
        "w_down", "b_down", "norm_ple", "w_ple_gate", "w_ple_proj", "norm_final"]
_OUTS = [(1, TP, D), (TS, 1, D), (1, 1, H, P, P), (1, 1, HIST, QKV), (1, 1, CK - 1, CC),
         (1, TS, H, P, P), (1, TS, HIST, QKV), (1, TS, CK - 1, CC)]


def kernel(**inputs):
    import numpy as np
    import concourse.bacc as bacc
    from concourse.bass_utils import run_bass_kernel_spmd as run

    nc = bacc.Bacc("TRN2", target_bir_lowering=False, num_devices=1)
    arrays, aps, outs = {}, {}, []
    for name in _INS:
        x = np.ascontiguousarray(inputs[name])
        arrays["in_" + name] = x
        aps[name] = nc.dram_tensor("in_" + name, x.shape, FP32, kind="ExternalInput").ap()
    for i, shape in enumerate(_OUTS):
        outs.append(nc.dram_tensor(f"out_{i}", shape, FP32, kind="ExternalOutput").ap())
    build(nc, aps, outs)
    r = run(nc, [arrays], core_ids=[0])
    return tuple(r.results[0][f"out_{i}"] for i in range(len(_OUTS)))
```
